# Optimizing a Trainium2 kernel written in Bass

```python
import math
import jax, jax.numpy as jnp
from jax import lax
import numpy as np

D_MODEL = 2048
BATCH = 1
SEQ = 256
DEPTH = 1

HEAD_DIM = 128
N_MIX_HEADS = D_MODEL // HEAD_DIM
NSA_HEADS = N_MIX_HEADS // 2
NSA_KV_GROUPS = 2
NSA_HPG = NSA_HEADS // NSA_KV_GROUPS
NSA_CMP_STRIDE = 16
NSA_CMP_LEN = 2 * NSA_CMP_STRIDE
NSA_SEL_BLOCK = 64
NSA_TOPN = 16
NSA_WINDOW = 512
NSA_FORCE_BONUS = 1.0e4
MOBA_HEADS = N_MIX_HEADS - NSA_HEADS
MOBA_BLOCK = 256
MOBA_TOPK = 3
Q_BLK = 64
MEM_LEN = 256
XA_HEADS = 4
XA_DIM = 128
PEER_HEADS = 8
PEER_NKEYS = 128
PEER_NEXPERTS = PEER_NKEYS * PEER_NKEYS
PEER_QDIM = 256
PEER_TOPK = 16
PEER_TOK_BLK = 128
DN_ALPHA = (2 * DEPTH) ** 0.25
DN_BETA = (8 * DEPTH) ** -0.25
LN_EPS = 1e-5

NSA_Q_COLS = NSA_HEADS * HEAD_DIM
NSA_KV_COLS = NSA_KV_GROUPS * HEAD_DIM
NSA_GATE_COLS = NSA_HEADS * 3
MOBA_COLS = MOBA_HEADS * HEAD_DIM
IN_SPLITS = [NSA_Q_COLS] + [NSA_KV_COLS] * 6 + [NSA_GATE_COLS] + [MOBA_COLS] * 3
IN_COLS = sum(IN_SPLITS)

kernel_name = 'nsa_moba_peer_deepnorm_hybrid'

def _alibi_slopes():
    s = 2.0 ** (-8.0 * (np.arange(N_MIX_HEADS) + 1) / N_MIX_HEADS)
    s = s.astype(np.float32)
    return (jnp.asarray(s[0::2]).reshape(NSA_KV_GROUPS, NSA_HPG), jnp.asarray(s[1::2]))

def _layernorm(x, g, b):
    xf = x.astype(jnp.float32)
    mu = xf.mean(-1, keepdims=True)
    var = jnp.square(xf - mu).mean(-1, keepdims=True)
    return ((xf - mu) * lax.rsqrt(var + LN_EPS) * g.astype(jnp.float32) + b.astype(jnp.float32)).astype(x.dtype)

def _masked_softmax(s, mask):
    s = jnp.where(mask, s, -jnp.inf)
    m = jnp.max(s, -1, keepdims=True)
    m = jnp.where(jnp.isfinite(m), m, 0.0)
    e = jnp.where(mask, jnp.exp(s - m), 0.0)
    d = e.sum(-1, keepdims=True)
    return e / jnp.where(d > 0, d, 1.0)

def _gather_blocks(kb, idx):
    return jax.vmap(jax.vmap(lambda t, i: t[i]))(kb, idx)

def _compress(raw, pe, w1, w2):
    B, S, G, dk = raw.shape
    c = raw.reshape(B, S // NSA_CMP_STRIDE, NSA_CMP_STRIDE, G, dk)
    blocks = jnp.concatenate([c[:, :-1], c[:, 1:]], axis=2) + pe[:, None, :]
    hid = jax.nn.gelu(jnp.einsum('bnlgd,lde->bnge', blocks, w1))
    return jnp.einsum('bnge,ef->bgnf', hid, w2)

def _cmp_to_sel(p, n_sel):
    r = NSA_SEL_BLOCK // NSA_CMP_STRIDE
    nc = p.shape[-1]
    total = r * n_sel + 1
    pp = jnp.pad(p, [(0, 0)] * (p.ndim - 1) + [(1, total - nc - 1)])
    return pp[..., :r * n_sel].reshape(*p.shape[:-1], n_sel, r).sum(-1) + pp[..., r::r]

def _hybrid_mixer(x, w_in, pe_k, w1_k, w2_k, pe_v, w1_v, w2_v, w_out):
    B, S, _ = x.shape
    dt = x.dtype
    f32 = jnp.float32
    s_pad = -(-S // MOBA_BLOCK) * MOBA_BLOCK
    xp = jnp.pad(x, ((0, 0), (0, s_pad - S), (0, 0)))
    n_cmp = s_pad // NSA_CMP_STRIDE - 1
    n_sel = s_pad // NSA_SEL_BLOCK
    n_mb = s_pad // MOBA_BLOCK
    top_n = min(NSA_TOPN, n_sel)
    top_m = min(MOBA_TOPK, n_mb)
    G, HG, dk = NSA_KV_GROUPS, NSA_HPG, HEAD_DIM
    scale = HEAD_DIM ** -0.5
    slope_n, slope_m = _alibi_slopes()

    proj = jnp.einsum('bsd,de->bse', xp, w_in)
    nq, kc, vc, ks, vs, kw, vw, gl, mq, mk, mv = jnp.split(proj, list(np.cumsum(IN_SPLITS)[:-1]), axis=-1)

    nq = nq.reshape(B, s_pad, G, HG, dk).transpose(0, 2, 3, 1, 4) * scale
    kc = _compress(kc.reshape(B, s_pad, G, dk), pe_k, w1_k, w2_k)
    vc = _compress(vc.reshape(B, s_pad, G, dk), pe_v, w1_v, w2_v)
    cmp_end = jnp.arange(n_cmp) * NSA_CMP_STRIDE + (NSA_CMP_LEN - 1)
    heads_g = lambda a: a.reshape(B, s_pad, G, dk).transpose(0, 2, 1, 3)
    ks_blk = heads_g(ks).reshape(B, G, n_sel, NSA_SEL_BLOCK, dk)
    vs_blk = heads_g(vs).reshape(B, G, n_sel, NSA_SEL_BLOCK, dk)
    wpad = ((0, 0), (0, 0), (NSA_WINDOW, 0), (0, 0))
    kw = jnp.pad(heads_g(kw), wpad)
    vw = jnp.pad(heads_g(vw), wpad)
    gates = jax.nn.sigmoid(gl.astype(f32)).reshape(B, s_pad, NSA_HEADS, 3)

    heads_m = lambda a: a.reshape(B, s_pad, MOBA_HEADS, HEAD_DIM).transpose(0, 2, 1, 3)
    mq = heads_m(mq) * scale
    mk = heads_m(mk)
    mv = heads_m(mv)
    mk_blk = mk.reshape(B, MOBA_HEADS, n_mb, MOBA_BLOCK, HEAD_DIM)
    mv_blk = mv.reshape(B, MOBA_HEADS, n_mb, MOBA_BLOCK, HEAD_DIM)
    k_mean = mk_blk.mean(axis=3)

    def chunk(c):
        q0 = c * Q_BLK
        t = q0 + jnp.arange(Q_BLK)
        q = lax.dynamic_slice_in_dim(nq, q0, Q_BLK, axis=3)
        dist_c = (t[:, None] - cmp_end[None, :]).astype(f32)
        s_c = jnp.einsum('bghqd,bgnd->bghqn', q, kc).astype(f32) - slope_n[:, :, None, None] * dist_c
        p_c = _masked_softmax(s_c, cmp_end[None, :] <= t[:, None])
        o_c = jnp.einsum('bghqn,bgnd->bghqd', p_c.astype(dt), vc)
        imp = _cmp_to_sel(p_c.sum(axis=2), n_sel)
        j = jnp.arange(n_sel)[None, :]
        cur = (t // NSA_SEL_BLOCK)[:, None]
        forced = (j == 0) | (j == cur) | (j == cur - 1)
        sel_score = jnp.where(j * NSA_SEL_BLOCK <= t[:, None], imp + jnp.where(forced, NSA_FORCE_BONUS, 0.0), -jnp.inf)
        _, sel_idx = lax.top_k(sel_score, top_n)
        k_g = _gather_blocks(ks_blk, sel_idx)
        v_g = _gather_blocks(vs_blk, sel_idx)
        pos_s = sel_idx[..., None] * NSA_SEL_BLOCK + jnp.arange(NSA_SEL_BLOCK)
        dist_s = (t[None, None, :, None, None] - pos_s)[:, :, None]
        s_s = jnp.einsum('bghqd,bgqnkd->bghqnk', q, k_g).astype(f32) - slope_n[:, :, None, None, None] * dist_s.astype(f32)
        n_keys = top_n * NSA_SEL_BLOCK
        p_s = _masked_softmax(s_s.reshape(B, G, HG, Q_BLK, n_keys), (dist_s >= 0).reshape(B, G, 1, Q_BLK, n_keys))
        o_s = jnp.einsum('bghqk,bgqkd->bghqd', p_s.astype(dt), v_g.reshape(B, G, Q_BLK, n_keys, dk))
        k_w = lax.dynamic_slice_in_dim(kw, q0, NSA_WINDOW + Q_BLK, axis=2)
        v_w = lax.dynamic_slice_in_dim(vw, q0, NSA_WINDOW + Q_BLK, axis=2)
        pos_w = q0 - NSA_WINDOW + jnp.arange(NSA_WINDOW + Q_BLK)
        dist_w = t[:, None] - pos_w[None, :]
        m_w = (dist_w >= 0) & (dist_w < NSA_WINDOW) & (pos_w[None, :] >= 0)
        s_w = jnp.einsum('bghqd,bgkd->bghqk', q, k_w).astype(f32) - slope_n[:, :, None, None] * dist_w.astype(f32)
        p_w = _masked_softmax(s_w, m_w)
        o_w = jnp.einsum('bghqk,bgkd->bghqd', p_w.astype(dt), v_w)
        g = lax.dynamic_slice_in_dim(gates, q0, Q_BLK, axis=1).reshape(B, Q_BLK, G, HG, 3).transpose(0, 2, 3, 1, 4)
        o_nsa = (g[..., 0:1] * o_c + g[..., 1:2] * o_s + g[..., 2:3] * o_w).astype(dt)
        o_nsa = o_nsa.transpose(0, 3, 1, 2, 4).reshape(B, Q_BLK, NSA_Q_COLS)
        qm = lax.dynamic_slice_in_dim(mq, q0, Q_BLK, axis=2)
        cb = q0 // MOBA_BLOCK
        past = jnp.arange(n_mb) < cb
        gate = jnp.where(past, jnp.einsum('bhqd,bhnd->bhqn', qm, k_mean).astype(f32), -jnp.inf)
        _, bidx = lax.top_k(gate, top_m)
        valid = bidx < cb
        km_g = _gather_blocks(mk_blk, bidx)
        vm_g = _gather_blocks(mv_blk, bidx)
        pos_p = bidx[..., None] * MOBA_BLOCK + jnp.arange(MOBA_BLOCK)
        dist_p = (t[:, None, None] - pos_p).astype(f32)
        s_p = jnp.einsum('bhqd,bhqnkd->bhqnk', qm, km_g).astype(f32) - slope_m[:, None, None, None] * dist_p
        n_past = top_m * MOBA_BLOCK
        m_p = jnp.broadcast_to(valid[..., None], s_p.shape).reshape(B, MOBA_HEADS, Q_BLK, n_past)
        k_cur = lax.dynamic_slice_in_dim(mk, cb * MOBA_BLOCK, MOBA_BLOCK, axis=2)
        v_cur = lax.dynamic_slice_in_dim(mv, cb * MOBA_BLOCK, MOBA_BLOCK, axis=2)
        pos_c = cb * MOBA_BLOCK + jnp.arange(MOBA_BLOCK)
        dist_cur = t[:, None] - pos_c[None, :]
        s_cur = jnp.einsum('bhqd,bhkd->bhqk', qm, k_cur).astype(f32) - slope_m[:, None, None] * dist_cur.astype(f32)
        m_cur = jnp.broadcast_to(dist_cur >= 0, s_cur.shape)
        p_m = _masked_softmax(jnp.concatenate([s_p.reshape(B, MOBA_HEADS, Q_BLK, n_past), s_cur], -1),
                              jnp.concatenate([m_p, m_cur], -1)).astype(dt)
        o_m = (jnp.einsum('bhqk,bhqkd->bhqd', p_m[..., :n_past], vm_g.reshape(B, MOBA_HEADS, Q_BLK, n_past, HEAD_DIM))
               + jnp.einsum('bhqk,bhkd->bhqd', p_m[..., n_past:], v_cur))
        o_m = o_m.transpose(0, 2, 1, 3).reshape(B, Q_BLK, MOBA_COLS)
        return jnp.concatenate([o_nsa, o_m], axis=-1)

    out = lax.map(chunk, jnp.arange(s_pad // Q_BLK))
    out = out.transpose(1, 0, 2, 3).reshape(B, s_pad, NSA_Q_COLS + MOBA_COLS)[:, :S]
    return jnp.einsum('bse,ed->bsd', out, w_out)

def _memory_xattn(h, mem, w_q, w_kv, w_o):
    B, S, _ = h.shape
    M = mem.shape[1]
    q = jnp.einsum('bsd,de->bse', h, w_q).reshape(B, S, XA_HEADS, XA_DIM) * XA_DIM ** -0.5
    kv = jnp.einsum('bmd,de->bme', mem, w_kv).reshape(B, M, 2, XA_HEADS, XA_DIM)
    s = jnp.einsum('bshd,bmhd->bhsm', q, kv[:, :, 0]).astype(jnp.float32)
    p = jax.nn.softmax(s, axis=-1).astype(h.dtype)
    o = jnp.einsum('bhsm,bmhd->bshd', p, kv[:, :, 1]).reshape(B, S, XA_HEADS * XA_DIM)
    return jnp.einsum('bse,ed->bsd', o, w_o)

def _peer(h, w_q, sub_keys, exp_u, exp_v):
    B, S, D = h.shape
    dt = h.dtype
    T = B * S
    K = PEER_TOPK

    def block(xb):
        tb = xb.shape[0]
        q = jnp.einsum('td,de->te', xb, w_q).reshape(tb, PEER_HEADS, 2, PEER_QDIM // 2)
        s = jnp.einsum('thcd,hckd->thck', q, sub_keys).astype(jnp.float32)
        sv, si = lax.top_k(s, K)
        cand = (sv[:, :, 0, :, None] + sv[:, :, 1, None, :]).reshape(tb, PEER_HEADS, K * K)
        cidx = (si[:, :, 0, :, None] * PEER_NKEYS + si[:, :, 1, None, :]).reshape(tb, PEER_HEADS, K * K)
        top_v, top_j = lax.top_k(cand, K)
        eidx = jnp.take_along_axis(cidx, top_j, axis=-1)
        gw = jax.nn.softmax(top_v, axis=-1)
        u = exp_u[eidx]
        v = exp_v[eidx]
        a = jax.nn.gelu(jnp.einsum('td,thkd->thk', xb, u).astype(jnp.float32))
        return jnp.einsum('thk,thkd->td', (gw * a).astype(dt), v)

    out = lax.map(block, h.reshape(T // PEER_TOK_BLK, PEER_TOK_BLK, D))
    return out.reshape(B, S, D)

def setup_inputs(seed: int = 0) -> dict:
    key = jax.random.key(seed)
    ks = jax.random.split(key, 24)
    nrm = lambda k, shape, s: jax.random.normal(k, shape, jnp.float32) * s
    L = DEPTH
    return {
        'x': nrm(ks[0], (BATCH, SEQ, D_MODEL), 1.0),
        'mem': nrm(ks[1], (BATCH, MEM_LEN, D_MODEL), 1.0),
        'w_in': nrm(ks[2], (L, D_MODEL, IN_COLS), D_MODEL ** -0.5),
        'cmp_pe_k': nrm(ks[3], (L, NSA_CMP_LEN, HEAD_DIM), 0.1),
        'cmp_w1_k': nrm(ks[4], (L, NSA_CMP_LEN, HEAD_DIM, HEAD_DIM), (NSA_CMP_LEN * HEAD_DIM) ** -0.5),
        'cmp_w2_k': nrm(ks[5], (L, HEAD_DIM, HEAD_DIM), HEAD_DIM ** -0.5),
        'cmp_pe_v': nrm(ks[6], (L, NSA_CMP_LEN, HEAD_DIM), 0.1),
        'cmp_w1_v': nrm(ks[7], (L, NSA_CMP_LEN, HEAD_DIM, HEAD_DIM), (NSA_CMP_LEN * HEAD_DIM) ** -0.5),
        'cmp_w2_v': nrm(ks[8], (L, HEAD_DIM, HEAD_DIM), HEAD_DIM ** -0.5),
        'w_out': nrm(ks[9], (L, NSA_Q_COLS + MOBA_COLS, D_MODEL), DN_BETA * (NSA_Q_COLS + MOBA_COLS) ** -0.5),
        'ln1_g': 1.0 + nrm(ks[10], (L, D_MODEL), 0.01),
        'ln1_b': nrm(ks[11], (L, D_MODEL), 0.01),
        'xa_wq': nrm(ks[12], (L, D_MODEL, XA_HEADS * XA_DIM), D_MODEL ** -0.5),
        'xa_wkv': nrm(ks[13], (L, D_MODEL, 2 * XA_HEADS * XA_DIM), D_MODEL ** -0.5),
        'xa_wo': nrm(ks[14], (L, XA_HEADS * XA_DIM, D_MODEL), DN_BETA * (XA_HEADS * XA_DIM) ** -0.5),
        'ln2_g': 1.0 + nrm(ks[15], (L, D_MODEL), 0.01),
        'ln2_b': nrm(ks[16], (L, D_MODEL), 0.01),
        'peer_wq': nrm(ks[17], (L, D_MODEL, PEER_HEADS * PEER_QDIM), D_MODEL ** -0.5),
        'peer_subkeys': nrm(ks[18], (L, PEER_HEADS, 2, PEER_NKEYS, PEER_QDIM // 2), (PEER_QDIM // 2) ** -0.5),
        'peer_u': nrm(ks[19], (L, PEER_NEXPERTS, D_MODEL), D_MODEL ** -0.5),
        'peer_v': nrm(ks[20], (L, PEER_NEXPERTS, D_MODEL), DN_BETA),
        'ln3_g': 1.0 + nrm(ks[21], (L, D_MODEL), 0.01),
        'ln3_b': nrm(ks[22], (L, D_MODEL), 0.01),
    }

def reference(x, mem, w_in, cmp_pe_k, cmp_w1_k, cmp_w2_k, cmp_pe_v, cmp_w1_v, cmp_w2_v, w_out,
              ln1_g, ln1_b, xa_wq, xa_wkv, xa_wo, ln2_g, ln2_b,
              peer_wq, peer_subkeys, peer_u, peer_v, ln3_g, ln3_b):
    h = x
    for l in range(DEPTH):
        mix = _hybrid_mixer(h, w_in[l], cmp_pe_k[l], cmp_w1_k[l], cmp_w2_k[l],
                            cmp_pe_v[l], cmp_w1_v[l], cmp_w2_v[l], w_out[l])
        h = _layernorm(DN_ALPHA * h + mix, ln1_g[l], ln1_b[l])
        h = _layernorm(DN_ALPHA * h + _memory_xattn(h, mem, xa_wq[l], xa_wkv[l], xa_wo[l]), ln2_g[l], ln2_b[l])
        h = _layernorm(DN_ALPHA * h + _peer(h, peer_wq[l], peer_subkeys[l], peer_u[l], peer_v[l]), ln3_g[l], ln3_b[l])
    return h


_drawn_inputs = setup_inputs


def setup_inputs(seed=0):
    import zlib

    import numpy as np

    out = dict(_drawn_inputs(seed))
    spreads = {}
    factors = {'cmp_pe_k': 7.832, 'ln3_g': 5.529, 'ln3_b': 5.651}
    for name, (base, spread) in spreads.items():
        noise = np.random.default_rng([zlib.crc32(name.encode()), seed]).standard_normal(out[name].shape)
        drawn = base * np.exp(spread * noise) if base else spread * noise
        out[name] = __import__('jax').numpy.asarray(drawn.astype(out[name].dtype))
    for name, factor in factors.items():
        out[name] = (out[name] * factor).astype(out[name].dtype)
    return out
```

```python
from contextlib import ExitStack

import concourse.bass as bass
from concourse import mybir

F32 = mybir.dt.float32
F32R = mybir.dt.float32r
U32 = mybir.dt.uint32
ALU = mybir.AluOpType
ACT = mybir.ActivationFunctionType
AX_X = mybir.AxisListType.X

P = 128
T = 256
TT = T // P
D = 2048
KO = D // P
NQ = D // 512
HD = 128
NSA_H, MOBA_H, GROUPS = 8, 8, 2
CMP_STRIDE, CMP_LEN = 16, 32
N_CMP = T // CMP_STRIDE - 1
XA_H = 4
PEER_H, NKEYS, TOPK = 8, 128, 16
SCALE = float(HD) ** -0.5
ALPHA = 2.0 ** 0.25
EPS = 1e-5
MASKED = -1.0e30
TAKEN = -3.0e38
SLOPES = [2.0 ** (-(i + 1) / 2.0) for i in range(16)]

S_QK = 0
S_V = 32
S_GATE = 44
S_CMP = 45
S_WOUT = 49
S_XK = 65
S_XV = 69
S_XQ = 73
S_XO = 77
S_PQ = 81
S_PEER = 97
GROUPS_P = 16
PER_G = 16
N_SLOTS = S_PEER + GROUPS_P * PER_G
R = 4
AHEAD = R - 1

N_XK, N_XQ, N_PQ, N_U = 32, 36, 40, 56

B_KS, B_KW, B_NQ, B_MQ, B_MK = 0, 2, 4, 12, 20

A_X = 1
A_MIX = A_X + 16
A_MEM = A_MIX + 1
A_H1 = A_MEM + 8
A_XO = A_H1 + XA_H
A_H2 = A_XO + 8

UNITS = 2 * NSA_H + MOBA_H
QUAD = 4
STAGE_T = 32
SQ = STAGE_T // QUAD
N_STAGE = T // STAGE_T


class Steps:

    def __init__(self, eng, sem):
        self.eng, self.sem, self.n = eng, sem, 0

    def done(self, ins):
        ins.then_inc(self.sem, 1)
        self.n += 1

    def settle(self):
        self.eng.wait_ge(self.sem, self.n)


def build(nc, a):
    with ExitStack() as ctx:
        def sb(name, shape, dt=F32, c=ctx):
            return c.enter_context(nc.sbuf_tensor(name, shape, dt))

        def sem(name):
            return ctx.enter_context(nc.semaphore(name))

        bank = [ctx.enter_context(nc.psum_tensor(f"bank{i}", [P, 512], F32)) for i in range(8)]

        ring_raw = sb("ring_raw", [P, R, 2048])
        ring_hi = sb("ring_hi", [P, R, 2048], F32R)
        ring_lo = sb("ring_lo", [P, R, 2048], F32R)
        actT_hi = sb("actT_hi", [P, KO, T], F32R)
        actT_lo = sb("actT_lo", [P, KO, T], F32R)
        ident = sb("ident", [P, P])
        stats = sb("stats", [P, TT, NQ, 6])
        mv2 = sb("mv2", [P, TT, 2])
        rstd = sb("rstd", [P, TT])

        with ExitStack() as c0:
            act_raw = sb("act_raw", [P, KO, T], c=c0)
        with ExitStack() as c0:
            CW = T + 16
            cmpT_hi = sb("cmpT_hi", [P, 4, CW], F32R, c0)
            cmpT_lo = sb("cmpT_lo", [P, 4, CW], F32R, c0)
            hid_m = sb("hid_m", [P, NSA_H, P], F32, c0)
            hidT = sb("hidT", [P, 2, 32], F32, c0)
            pecol = sb("pecol", [P, 2], F32, c0)
            pe_raw = sb("pe_raw", [P, 2, 34], F32, c0)
            pe_hi = sb("pe_hi", [P, 2, 34], F32R, c0)
            pe_lo = sb("pe_lo", [P, 2, 34], F32R, c0)
            w2 = sb("w2", [P, 2, P], F32, c0)
        hres = sb("hres", [P, TT, D])

        with ExitStack() as c1:
            qkT = sb("qkT", [P, 28, T], c=c1)
            vN = sb("vN", [P, TT, 1536], c=c1)
            dist = sb("dist", [P, 384], c=c1)
            distc = sb("distc", [P, TT, NSA_H, 16], c=c1)
            maskc = sb("maskc", [P, TT, NSA_H, 16], c=c1)
            z = sb("z", [P, 2, 384], c=c1)
            pT = sb("pT", [P, 2, 384], c=c1)
            zc = sb("zc", [P, TT, NSA_H, 16], c=c1)
            pc = sb("pc", [P, TT, NSA_H, 16], c=c1)
            pcT = sb("pcT", [P, T], c=c1)
            vcm = sb("vcm", [P, NSA_H, P], c=c1)
            kcT = sb("kcT", [P, 32], c=c1)
            gates = sb("gates", [P, TT, NSA_H, 3], c=c1)
            mc = sb("mc", [P, TT, NSA_H], c=c1)
            dc = sb("dc", [P, TT, NSA_H], c=c1)
            mx = sb("mx", [P, 2, 2], c=c1)
            nm = sb("nm", [P, 2, 2], c=c1)
            rs = sb("rs", [P, 2, 2], c=c1)
            rr = sb("rr", [P, 2, 2], c=c1)
        with ExitStack() as c1:
            gb = sb("gb", [P, 2, D], c=c1)
            mem_raw = sb("mem_raw", [P, KO, T], c=c1)
            xk = sb("xk", [P, XA_H, T], c=c1)
            xv = sb("xv", [P, TT, 512], c=c1)
            xq = sb("xq", [P, XA_H, T], c=c1)
            xp = sb("xp", [P, XA_H, 512], c=c1)
            xpT = sb("xpT", [P, 2, 512], c=c1)
            xm = sb("xm", [P, XA_H, 2], c=c1)
            xr = sb("xr", [P, XA_H, 2], c=c1)
        with ExitStack() as c2:
            idxT = sb("idxT", [P, 3, T], c=c2)
            iota_row = sb("iota_row", [P, P], c=c2)
            with ExitStack() as c3:
                pq = sb("pq", [P, 16, T], c=c3)
                subk = sb("subk", [P, 16, P], c=c3)
                sc = sb("sc", [P, TT, 16, P], c=c3)
                tmp = sb("tmp", [P, 16, P], c=c3)
                sv = sb("sv", [P, 16, TOPK], c=c3)
                si = sb("si", [P, 16, TOPK], U32, c3)
                sif = sb("sif", [P, 16, TOPK], F32, c3)
                tv = sb("tv", [P, PEER_H, TOPK], c=c3)
                tj = sb("tj", [P, PEER_H, TOPK], U32, c3)
                tji = sb("tji", [P, 2, PEER_H, TOPK], U32, c3)
                tjf = sb("tjf", [P, 2, PEER_H, TOPK], F32, c3)
                pick = sb("pick", [P, 3, PEER_H, TOPK], c=c3)
                gsum = sb("gsum", [P, PEER_H], c=c3)
            with ExitStack() as c3:
                oh1 = sb("oh1", [P, 2, QUAD, P], c=c3)
                oh2 = sb("oh2", [P, 2, QUAD, P], c=c3)
                stage = sb("stage", [P, 2, P, STAGE_T], c=c3)
        with ExitStack() as c2:
            gb3 = sb("gb3", [P, 2, D], c=c2)
            w_hi = sb("w_hi", [P, 8, T], F32R, c2)
            w_lo = sb("w_lo", [P, 8, T], F32R, c2)
            gbuf = sb("gbuf", [P, 2, N_STAGE, 4, STAGE_T], F32, c2)
            ga = sb("ga", [P, 2, T], c=c2)
            wt = sb("wt", [P, 2, T], c=c2)

        cand = pq[:, 0:8, :].rearrange("p h (i j) -> p h i j", i=TOPK)
        hot = pq[:, 8:16, :].rearrange("p h (i j) -> p h i j", i=TOPK)

        landed = [sem(f"landed{r}") for r in range(R)]
        hi_ready = sem("hi_ready")
        lo_ready = sem("lo_ready")
        slots_done = sem("slots_done")
        tb_out = sem("tb_out")
        cmp_lo = sem("cmp_lo")
        act_nb = sem("act_nb")
        dve_nb = sem("dve_nb")
        x_landed = sem("x_landed")
        const_landed = sem("const_landed")
        mem_landed = sem("mem_landed")
        res_landed = sem("res_landed")
        gb_landed = sem("gb_landed")
        subk_landed = sem("subk_landed")
        act_hi = sem("act_hi")
        act_lo = sem("act_lo")
        pool_step = sem("pool_step")
        consts = sem("consts")
        dve_step = sem("dve_step")
        act_step = sem("act_step")
        gate_exp = sem("gate_exp")
        gate_ready = sem("gate_ready")
        pe_split = sem("pe_split")
        hid_ready = sem("hid_ready")
        hidm_ready = sem("hidm_ready")
        kc_psum = sem("kc_psum")
        kc_ready = sem("kc_ready")
        vc_psum = sem("vc_psum")
        vc_ready = sem("vc_ready")
        sc_psum = sem("sc_psum")
        zc_ready = sem("zc_ready")
        ec_ready = sem("ec_ready")
        pc_ready = sem("pc_ready")
        pct_psum = sem("pct_psum")
        pct_ready = sem("pct_ready")
        s_ready = sem("s_ready")
        z_done = sem("z_done")
        mx_done = sem("mx_done")
        nm_ready = sem("nm_ready")
        e_done = sem("e_done")
        rs_done = sem("rs_done")
        p_ready = sem("p_ready")
        pt_done = sem("pt_done")
        pt_out = sem("pt_out")
        pv_done = sem("pv_done")
        var_ready = sem("var_ready")
        rstd_ready = sem("rstd_ready")
        ln_ready = sem("ln_ready")
        ht_done = sem("ht_done")
        xs_ready = sem("xs_ready")
        xm_ready = sem("xm_ready")
        xe_done = sem("xe_done")
        xp_ready = sem("xp_ready")
        xt_done = sem("xt_done")
        xt_out = sem("xt_out")
        xo_done = sem("xo_done")
        key_psum = sem("key_psum")
        key_out = sem("key_out")
        tv_ready = sem("tv_ready")
        te_done = sem("te_done")
        pick_ready = sem("pick_ready")
        idx_psum = sem("idx_psum")
        idx_out = sem("idx_out")
        oh1_ready = sem("oh1_ready")
        oh2_ready = sem("oh2_ready")
        g_mm = sem("g_mm")
        g_out = sem("g_out")
        stage_out = [sem(f"stage_out{i}") for i in range(2)]
        g_landed = [sem(f"g_landed{i}") for i in range(2)]
        w_mul = sem("w_mul")
        w_high = sem("w_high")
        w_ready = sem("w_ready")
        stored = sem("stored")

        gdram = nc.dram_tensor("gate_matrix", (P, N_STAGE, P, STAGE_T), F32, kind="Internal").ap()

        block = ctx.enter_context(nc.Block())

        @block.sync
        def _(sp):
            for s in range(R):
                sp.dma_start(ring_raw[:, s, :], a["stream"][s]).then_inc(landed[s], 16)
            rounds = (N_SLOTS - R) // R
            with sp.Fori(0, rounds) as i:
                for r in range(R):
                    sp.wait_ge(lo_ready, i * R + (r + 1))
                    sp.dma_start(ring_raw[:, r, :], a["stream"][i * R + (R + r)]).then_inc(landed[r], 16)
            for s in range(R + rounds * R, N_SLOTS):
                sp.wait_ge(lo_ready, s - R + 1)
                sp.dma_start(ring_raw[:, s % R, :], a["stream"][s]).then_inc(landed[s % R], 16)
            for t in range(TT):
                sp.wait_ge(ln_ready, 2 * TT + t + 1)
                sp.dma_start(a["out"][t * P:(t + 1) * P, :], hres[:, t, :]).then_inc(stored, 16)
            sp.wait_ge(stored, 16 * TT)

        @block.gpsimd
        def _(pool):
            st = Steps(pool, pool_step)
            pool.dma_start(act_raw[:], a["xT"]).then_inc(x_landed, 16)
            st.done(pool.memset(ident[:], 0.0))
            st.done(pool.iota(dist[:, 0:P], [[1, P]], base=0, channel_multiplier=-1, allow_small_or_imprecise_dtypes=True))
            st.done(pool.iota(dist[:, P:384], [[1, T]], base=-P, channel_multiplier=-1, allow_small_or_imprecise_dtypes=True))
            st.done(pool.iota(distc[:], [[-P, TT], [0, NSA_H], [CMP_STRIDE, 16]], base=CMP_LEN - 1, channel_multiplier=-1,
                              allow_small_or_imprecise_dtypes=True))
            st.done(pool.memset(maskc[:], 1.0))
            st.settle()
            st.done(pool.affine_select(out=ident[:], in_=ident[:], compare_op=ALU.not_equal, fill=1.0, base=0,
                                       pattern=[[-1, P]], channel_multiplier=1))
            st.done(pool.affine_select(out=dist[:, 0:P], in_=dist[:, 0:P], compare_op=ALU.is_ge, fill=MASKED, base=0,
                                       pattern=[[-1, P]], channel_multiplier=1))
            st.done(pool.affine_select(out=dist[:, P:384], in_=dist[:, P:384], compare_op=ALU.is_ge, fill=MASKED, base=P,
                                       pattern=[[-1, T]], channel_multiplier=1))
            for ap, fill in ((distc, MASKED), (maskc, 0.0)):
                st.done(pool.affine_select(out=ap[:], in_=ap[:], compare_op=ALU.is_ge, fill=fill, base=-(CMP_LEN - 1),
                                           pattern=[[P, TT], [0, NSA_H], [-CMP_STRIDE, 16]], channel_multiplier=1))
            st.settle()
            for h in range(NSA_H):
                pool.tensor_scalar(distc[:, :, h, :], distc[:, :, h, :], SLOPES[2 * h] / SCALE, None, ALU.mult).then_inc(consts, 1)
            pool.wait_ge(act_lo, A_X)
            pool.dma_start(pe_raw[:], a["peT"]).then_inc(const_landed, 16)
            pool.dma_start(w2[:], a["w2"]).then_inc(const_landed, 16)
            pool.wait_ge(vc_psum, 2)
            pool.wait_ge(hidm_ready, 1)
            pool.dma_start(hres[:], a["x"]).then_inc(res_landed, 16)
            pool.wait_ge(act_lo, A_MIX)
            pool.dma_start(mem_raw[:], a["memT"]).then_inc(mem_landed, 16)
            for k in range(2):
                if k:
                    pool.wait_ge(ln_ready, TT)
                for j, name in enumerate((f"ln{k + 1}_g", f"ln{k + 1}_b")):
                    pool.dma_start(gb[:, j, :], a[name].partition_broadcast(P)).then_inc(gb_landed, 16)
            pool.wait_ge(ln_ready, 2 * TT)
            pool.dma_start(subk[:], a["subkT"]).then_inc(subk_landed, 16)
            pool.iota(iota_row[:], [[1, P]], base=0, channel_multiplier=0, allow_small_or_imprecise_dtypes=True).then_inc(consts, 1)
            pool.wait_ge(consts, NSA_H + 1)
            for b in range(2):
                pool.wait_ge(stage_out[b], 16 * (N_STAGE // 2))

            def load_gates(first_key, b):
                src = gdram[:, :, bass.ds(first_key, 4), :]
                pool.dma_start(gbuf[:, b], src).then_inc(g_landed[b], 16)

            for b in range(2):
                load_gates(4 * b, b)
            for j, name in enumerate(("ln3_g", "ln3_b")):
                pool.dma_start(gb3[:, j, :], a[name].partition_broadcast(P)).then_inc(gb_landed, 16)
            with pool.Fori(1, GROUPS_P) as g:
                for b in range(2):
                    pool.wait_ge(w_mul, g * 8 + (4 * b - 2))
                    load_gates(g * 8 + 4 * b, b)

        @block.tensor
        def _(pe):
            PASSES = ((0, 0), (0, 1), (1, 0))
            ring = (ring_hi, ring_lo)
            act = (actT_hi, actT_lo)

            def block_slot(s, r, out, want_act=None):
                pe.wait_ge(lo_ready, s + 1)
                for k in range(KO):
                    for n, (w, x) in enumerate(PASSES):
                        last = pe.matmul(out[:, 0:T], ring[w][:, r, k * P:(k + 1) * P], act[x][:, k, :],
                                         start=(k == 0 and n == 0), stop=(k == KO - 1 and n == 2))
                last.then_inc(slots_done, 1)

            def row_slot(s, q, nq, outs):
                r = s % R
                pe.wait_ge(lo_ready, s + 1)
                for t in range(TT):
                    for j in range(4):
                        k = 4 * q + j
                        for n, (x, w) in enumerate(PASSES):
                            last = pe.matmul(outs[t][:, :], act[x][:, k, t * P:(t + 1) * P],
                                             ring[w][:, r, j * 512:(j + 1) * 512],
                                             start=(q == 0 and j == 0 and n == 0),
                                             stop=(q == nq - 1 and j == 3 and n == 2))
                last.then_inc(slots_done, 1)

            def pair(m):
                return bank[2 + 2 * (m % 2)], bank[3 + 2 * (m % 2)]

            pe.wait_ge(act_lo, A_X)
            for n in range(4):
                if n >= 2:
                    pe.wait_ge(tb_out, n - 1)
                    pe.wait_ge(cmp_lo, n - 1)
                block_slot(n, n, bank[n % 2])
            pe.wait_ge(cmp_lo, 4)
            with pe.Fori(1, 8) as i:
                for r in range(4):
                    pe.wait_ge(tb_out, i * 4 + (r - 1))
                    block_slot(i * 4 + r, r, bank[r % 2])
            for m in range(3):
                if m == 2:
                    pe.wait_ge(act_nb, 2)
                for q in range(4):
                    row_slot(S_V + 4 * m + q, q, 4, pair(m))
            pe.wait_ge(lo_ready, S_GATE + 1)
            for t in range(TT):
                for k in range(KO):
                    for n, (x, w) in enumerate(PASSES):
                        last = pe.matmul(bank[6][:, t * 24:(t + 1) * 24], act[x][:, k, t * P:(t + 1) * P],
                                         ring[w][:, S_GATE % R, k * 24:(k + 1) * 24],
                                         start=(k == 0 and n == 0), stop=(k == KO - 1 and n == 2))
            last.then_inc(slots_done, 1)
            pe.wait_ge(pe_split, 2)
            pe.wait_ge(tb_out, 32)
            cmp_parts, pe_parts = (cmpT_hi, cmpT_lo), (pe_hi, pe_lo)
            for kv in range(2):
                out = bank[7 * (1 - kv)]
                for half in range(2):
                    s = S_CMP + 2 * kv + half
                    pe.wait_ge(lo_ready, s + 1)
                    for j in range(16):
                        l = 16 * half + j
                        for n, (w, x) in enumerate(PASSES):
                            lhsT = ring[w][:, s % R, j * P:(j + 1) * P]
                            tokens = cmp_parts[x][:, 2 * kv:2 * kv + 2, l:l + 16 * 15 + 1:16]
                            pe.matmul(out[:, 0:32], lhsT, tokens, start=(l == 0 and n == 0), stop=(l == 31 and n == 2),
                                      skip_group_check=True)
                            last = pe.matmul(out[:, 32:34], lhsT, pe_parts[x][:, kv, l:l + 2], start=False,
                                             stop=(l == 31 and n == 2), skip_group_check=True)
                    last.then_inc(slots_done, 1)
            pe.wait_ge(const_landed, 32)
            pe.wait_ge(hid_ready, 1)
            pe.matmul(bank[1][:, 0:32], w2[:, 0, :], hidT[:, 0, :], start=True, stop=True).then_inc(kc_psum, 1)
            pe.wait_ge(hidm_ready, 1)
            pe.wait_ge(act_nb, 6)
            for h in range(NSA_H):
                last = pe.matmul(bank[4 + h // 4][:, (h % 4) * P:(h % 4 + 1) * P], hid_m[:, h, :], w2[:, 1, :],
                                 start=True, stop=True)
                if h % 4 == 3:
                    last.then_inc(vc_psum, 1)
            pe.wait_ge(kc_ready, 1)
            pe.wait_ge(hid_ready, 2)
            for t in range(TT):
                for h in range(NSA_H):
                    g = h // 4
                    c = (t * NSA_H + h) * 16
                    last = pe.matmul(bank[0][:, c:c + 16], qkT[:, B_NQ + h, t * P:(t + 1) * P], kcT[:, 16 * g:16 * g + 16],
                                     start=True, stop=True)
            last.then_inc(sc_psum, 1)

            units = causal_units()

            def scores(u):
                qb, kb, _, _ = units[u]
                out = bank[4 + u % 2]
                pe.matmul(out[:, 0:P], qkT[:, qb, 0:P], qkT[:, kb, 0:P], start=True, stop=True)
                pe.matmul(out[:, P:384], qkT[:, qb, P:T], qkT[:, kb, :], start=True, stop=True).then_inc(s_ready, 1)

            def turn(u):
                pe.wait_ge(p_ready, 2 * (u + 1))
                if u >= 2:
                    pe.wait_ge(pt_out, u - 1)
                for i in range(3):
                    last = pe.transpose(bank[6 + u % 2][:, i * P:(i + 1) * P], z[:, u % 2, i * P:(i + 1) * P], ident[:])
                last.then_inc(pt_done, 1)

            def weigh(u):
                _, _, h, vcol = units[u]
                out = bank[2 + h % 2]
                first = u < 2 * NSA_H and u % 2 == 0
                if h >= 2 and (first or h >= NSA_H):
                    pe.wait_ge(act_lo, A_X + h - 1)
                if first:
                    pe.wait_ge(pct_ready, 1)
                    pe.matmul(out[:, 0:T], vcm[:, h, :], pcT[:], start=True, stop=False, skip_group_check=True)
                pe.wait_ge(pt_out, u + 1)
                pe.matmul(out[:, 0:T], vN[:, 0, vcol:vcol + P], pT[:, u % 2, 0:T], start=(h >= NSA_H), stop=False,
                          skip_group_check=True)
                pe.matmul(out[:, P:T], vN[:, 1, vcol:vcol + P], pT[:, u % 2, T:384], start=False, stop=True,
                          skip_group_check=True).then_inc(pv_done, 1)

            pe.wait_ge(vc_ready, 2)
            scores(0)
            scores(1)
            pe.wait_ge(pc_ready, 1)
            pe.wait_ge(kc_ready, 1)
            for t in range(TT):
                last = pe.transpose(bank[1][:, t * P:(t + 1) * P], pc[:, t].rearrange("p h n -> p (h n)"), ident[:])
            last.then_inc(pct_psum, 1)
            for u in range(UNITS):
                turn(u)
                if u + 2 < UNITS:
                    pe.wait_ge(z_done, u + 1)
                    scores(u + 2)
                if u:
                    weigh(u - 1)
            weigh(UNITS - 1)

            pe.wait_ge(act_lo, A_MIX)
            for j in range(NQ):
                m = 3 + j
                if j >= 2:
                    pe.wait_ge(dve_nb, 2 * (j - 1))
                for q in range(4):
                    row_slot(S_WOUT + 4 * j + q, q, 4, pair(m))
            pe.wait_ge(act_lo, A_MEM)
            for b in range(XA_H):
                pe.wait_ge(tb_out, N_XK + b - 1)
                pe.wait_ge(pct_ready, 1)
                block_slot(S_XK + b, (S_XK + b) % R, bank[b % 2])
            pe.wait_ge(dve_nb, 6)
            for q in range(4):
                row_slot(S_XV + q, q, 4, pair(7))

            def turn_residual():
                for t in range(TT):
                    for kq in range(4):
                        c = 4 * t + kq
                        if kq == 0:
                            pe.wait_ge(ln_ready, ln_base + t + 1)
                        for i in range(4):
                            k = 4 * kq + i
                            last = pe.transpose(bank[(6 + c) % 8][:, i * P:(i + 1) * P], hres[:, t, k * P:(k + 1) * P], ident[:])
                        last.then_inc(ht_done, 1)

            pe.wait_ge(tb_out, N_XQ)
            pe.wait_ge(act_nb, 8)
            ln_base = 0
            turn_residual()
            pe.wait_ge(act_lo, A_H1)
            for b in range(XA_H):
                if b >= 2:
                    pe.wait_ge(tb_out, N_XQ + b - 1)
                block_slot(S_XQ + b, (S_XQ + b) % R, bank[b % 2])
            pe.wait_ge(tb_out, N_PQ)
            for h in range(XA_H):
                for t in range(TT):
                    last = pe.matmul(bank[2 + h][:, t * T:(t + 1) * T], xq[:, h, t * P:(t + 1) * P], xk[:, h, :],
                                     start=True, stop=True)
                last.then_inc(xs_ready, 1)
            for h in range(XA_H):
                pe.wait_ge(xp_ready, 2 * (h + 1))
                if h >= 2:
                    pe.wait_ge(xt_out, h - 1)
                for kb in range(2):
                    for t in range(TT):
                        c = kb * T + t * P
                        last = pe.transpose(bank[6 + h % 2][:, c:c + P], xp[:, h, t * T + kb * P:t * T + kb * P + P], ident[:])
                last.then_inc(xt_done, 1)
                pe.wait_ge(xt_out, h + 1)
                if h >= 2:
                    pe.wait_ge(act_lo, A_H1 + h - 1)
                for kb in range(2):
                    last = pe.matmul(bank[h % 2][:, 0:T], xv[:, kb, h * HD:(h + 1) * HD], xpT[:, h % 2, kb * T:(kb + 1) * T],
                                     start=(kb == 0), stop=(kb == 1))
                last.then_inc(xo_done, 1)
            pe.wait_ge(act_lo, A_XO)
            for j in range(NQ):
                if j >= 2:
                    pe.wait_ge(dve_nb, 8 + 2 * (j - 1))
                row_slot(S_XO + j, 0, 1, pair(8 + j))
            ln_base = TT
            turn_residual()
            pe.wait_ge(act_lo, A_H2)
            for b in range(16):
                pe.wait_ge(tb_out, N_PQ + b - 1)
                block_slot(S_PQ + b, (S_PQ + b) % R, bank[b % 2])
            pe.wait_ge(tb_out, N_U)
            pe.wait_ge(subk_landed, 16)
            for t in range(TT):
                for b in range(16):
                    last = pe.matmul(bank[4 * (1 - t) + b // 4][:, (b % 4) * P:(b % 4 + 1) * P], pq[:, b, t * P:(t + 1) * P],
                                     subk[:, b, :], start=True, stop=True)
                last.then_inc(key_psum, 1)
            for t in range(TT):
                pe.wait_ge(pick_ready, t + 1)
                pe.wait_ge(key_out, 2)
                for c in range(3):
                    last = pe.transpose(bank[2 + t][:, c * P:(c + 1) * P], pick[:, c].rearrange("p h k -> p (h k)"), ident[:])
                last.then_inc(idx_psum, 1)
            pe.wait_ge(idx_out, 2)
            pe.sem_inc(g_mm, 2)
            with pe.Fori(0, N_STAGE // 2) as i:
                for q in range(2 * SQ):
                    n = i * (2 * SQ) + q
                    pe.wait_ge(oh1_ready, n + 1)
                    pe.wait_ge(oh2_ready, n + 1)
                    pe.wait_ge(g_out, n + 1)
                    for j in range(QUAD):
                        last = pe.matmul(bank[4 + q % 4][:, j * P:(j + 1) * P], oh2[:, q % 2, j, :], oh1[:, q % 2, j, :],
                                         start=True, stop=True)
                    last.then_inc(g_mm, 1)
            w_part = (w_hi, w_lo)
            with pe.Fori(0, GROUPS_P) as g:
                for c in range(8):
                    pe.wait_ge(tb_out, g * 8 + (N_U + c - 1))
                    block_slot(g * PER_G + (S_PEER + c), (S_PEER + c) % R, bank[c % 2])
                for j in range(NQ):
                    outs = pair(j)
                    pe.wait_ge(dve_nb, g * 8 + (16 + 2 * (j - 1)))
                    for half in range(2):
                        s0 = S_PEER + 8 + 2 * j + half
                        pe.wait_ge(lo_ready, g * PER_G + (s0 + 1))
                        for c4 in range(4):
                            c = 4 * half + c4
                            if j == 0:
                                pe.wait_ge(w_ready, g * 8 + (c + 1))
                            for t in range(TT):
                                for n, (x, w) in enumerate(PASSES):
                                    last = pe.matmul(outs[t][:, :], w_part[x][:, c, t * P:(t + 1) * P],
                                                     ring[w][:, s0 % R, c4 * 512:(c4 + 1) * 512],
                                                     start=(c == 0 and n == 0), stop=(c == 7 and n == 2))
                        last.then_inc(slots_done, 1)

        @block.scalar
        def _(act):
            st = Steps(act, act_step)

            def high(s, lap=None):
                r, laps = s % R, 16 * (s // R + 1)
                act.wait_ge(landed[r], laps if lap is None else lap * (16 // R) + laps)
                if lap is not None:
                    act.wait_ge(slots_done, lap + (s - AHEAD))
                elif s >= R:
                    act.wait_ge(slots_done, s - AHEAD)
                act.copy(ring_hi[:, r, :], ring_raw[:, r, :]).then_inc(hi_ready, 1)

            def deviation(n):
                act.wait_ge(var_ready, n)
                act.activation(rstd[:], rstd[:], ACT.Sqrt).then_inc(rstd_ready, 1)

            def rows_out(s, m, dst):
                act.wait_ge(slots_done, s + 1)
                for t in range(TT):
                    act.copy(dst(t), bank[2 + 2 * (m % 2) + t][:, :]).then_inc(act_nb, 1)

            high(0)
            act.wait_ge(x_landed, 16)
            act.copy(actT_hi[:], act_raw[:]).then_inc(act_hi, 1)
            high(1)
            high(2)
            for s in range(4):
                high(s + AHEAD)
                act.wait_ge(slots_done, s + 1)
                if s == 0:
                    act.wait_ge(act_lo, A_X)
                act.copy(cmpT_hi[:, s, 0:T], bank[s % 2][:, 0:T]).then_inc(tb_out, 1)
            with act.Fori(1, 8) as i:
                for r in range(4):
                    high(r + AHEAD, i * 4)
                    act.wait_ge(slots_done, i * 4 + (r + 1))
                    act.copy(qkT[:, i * 4 + (r - 4), :], bank[r % 2][:, 0:T]).then_inc(tb_out, 1)
            for s in range(S_V, S_GATE):
                high(s + AHEAD)
                if s % 4 == 3:
                    m = (s - S_V) // 4
                    rows_out(s, m, lambda t: vN[:, t, 512 * m:512 * (m + 1)])
            high(S_GATE + AHEAD)
            act.wait_ge(slots_done, S_GATE + 1)
            act.activation(gates[:].rearrange("p t h b -> p (t h b)"), bank[6][:, 0:48], ACT.Exp, scale=-1.0).then_inc(gate_exp, 1)
            act.wait_ge(const_landed, 32)
            act.copy(pe_hi[:], pe_raw[:]).then_inc(pe_split, 1)
            for kv in range(2):
                for half in range(2):
                    s = S_CMP + 2 * kv + half
                    high(s + AHEAD)
                act.wait_ge(slots_done, S_CMP + 2 * kv + 2)
                out = bank[7 * (1 - kv)]
                st.done(act.copy(pecol[:, kv:kv + 1], out[:, 32:33]))
                st.settle()
                act.activation(hidT[:, kv, :], out[:, 0:32], ACT.Gelu_apprx_tanh, bias=pecol[:, kv:kv + 1]).then_inc(hid_ready, 1)
            act.wait_ge(kc_psum, 1)
            act.copy(kcT[:], bank[1][:, 0:32]).then_inc(kc_ready, 1)
            for b in range(2):
                act.wait_ge(vc_psum, b + 1)
                act.copy(vcm[:, 4 * b:4 * b + 4, :].rearrange("p h d -> p (h d)"), bank[4 + b][:, :]).then_inc(vc_ready, 1)
            act.wait_ge(zc_ready, 1)
            act.activation(pc[:], zc[:], ACT.Exp, scale=SCALE).then_inc(ec_ready, 1)

            units = causal_units()

            def exponentials(u):
                act.wait_ge(nm_ready, u + 1)
                for t, (c0, c1) in enumerate(((0, P), (P, 384))):
                    act.activation(z[:, u % 2, c0:c1], z[:, u % 2, c0:c1], ACT.Exp, bias=nm[:, u % 2, t:t + 1], scale=SCALE,
                                   accum_out=rs[:, u % 2, t:t + 1]).then_inc(e_done, 1)

            def turned_out(u):
                act.wait_ge(pt_done, u + 1)
                if u >= 2:
                    act.wait_ge(pv_done, u - 1)
                act.copy(pT[:, u % 2, :], bank[6 + u % 2][:, 0:384]).then_inc(pt_out, 1)

            def head_high(u):
                h = units[u][2]
                if u >= 2 * NSA_H or u % 2:
                    act.wait_ge(pv_done, u + 1)
                    act.copy(actT_hi[:, h, :], bank[2 + h % 2][:, 0:T]).then_inc(act_hi, 1)

            for u in range(UNITS + 2):
                if u < UNITS:
                    exponentials(u)
                if u == 0:
                    act.wait_ge(pct_psum, 1)
                    act.copy(pcT[:], bank[1][:, 0:T]).then_inc(pct_ready, 1)
                if 1 <= u <= UNITS:
                    turned_out(u - 1)
                if u >= 2:
                    head_high(u - 2)
            for s in range(S_WOUT, S_XK):
                high(s + AHEAD)
            act.wait_ge(mem_landed, 16)
            act.wait_ge(slots_done, S_XK)
            act.copy(actT_hi[:], mem_raw[:]).then_inc(act_hi, 1)
            for b in range(XA_H):
                s = S_XK + b
                high(s + AHEAD)
                if b == 0:
                    deviation(1)
                act.wait_ge(slots_done, s + 1)
                act.copy(xk[:, b, :], bank[b % 2][:, 0:T]).then_inc(tb_out, 1)
            for q in range(4):
                high(S_XV + q + AHEAD)
            rows_out(S_XV + 3, 7, lambda t: xv[:, t, :])

            def residual_high(first):
                for t in range(TT):
                    for kq in range(4):
                        c = 4 * t + kq
                        act.wait_ge(ht_done, first + c + 1)
                        act.copy(actT_hi[:, 4 * kq:4 * kq + 4, t * P:(t + 1) * P],
                                 bank[(6 + c) % 8][:].rearrange("p (k t) -> p k t", k=4)).then_inc(act_hi, 1)

            residual_high(0)
            for b in range(XA_H):
                s = S_XQ + b
                high(s + AHEAD)
                act.wait_ge(slots_done, s + 1)
                act.copy(xq[:, b, :], bank[b % 2][:, 0:T]).then_inc(tb_out, 1)
            for h in range(XA_H):
                act.wait_ge(xm_ready, h + 1)
                for t in range(TT):
                    act.activation(xp[:, h, t * T:(t + 1) * T], bank[2 + h][:, t * T:(t + 1) * T], ACT.Exp,
                                   bias=xm[:, h, t:t + 1], scale=SCALE, accum_out=xr[:, h, t:t + 1]).then_inc(xe_done, 1)
            for h in range(XA_H):
                act.wait_ge(xt_done, h + 1)
                if h >= 2:
                    act.wait_ge(xo_done, h - 1)
                act.copy(xpT[:, h % 2, :], bank[6 + h % 2][:, :]).then_inc(xt_out, 1)
                act.wait_ge(xo_done, h + 1)
                act.copy(actT_hi[:, h, :], bank[h % 2][:, 0:T]).then_inc(act_hi, 1)
            for j in range(NQ):
                high(S_XO + j + AHEAD)
            deviation(2)
            residual_high(8)
            for b in range(16):
                s = S_PQ + b
                high(s + AHEAD)
                act.wait_ge(slots_done, s + 1)
                act.copy(pq[:, b, :], bank[b % 2][:, 0:T]).then_inc(tb_out, 1)
            for t in range(TT):
                act.wait_ge(key_psum, t + 1)
                for i in range(4):
                    ins = act.copy(sc[:, t, 4 * i:4 * i + 4, :].rearrange("p b k -> p (b k)"), bank[4 * (1 - t) + i][:, :])
                ins.then_inc(key_out, 1)
            for t in range(TT):
                act.wait_ge(tv_ready, t + 1)
                act.activation(pick[:, 2], tv[:], ACT.Exp).then_inc(te_done, 1)
            for t in range(TT):
                act.wait_ge(idx_psum, t + 1)
                act.copy(idxT[:, :, t * P:(t + 1) * P], bank[2 + t][:, 0:384].rearrange("p (c t) -> p c t", c=3)).then_inc(idx_out, 1)
            act.sem_inc(g_out, 4)

            def stages(i, first):
                for b in range(2):
                    if not first:
                        act.wait_ge(stage_out[b], i * 16)
                    for q8 in range(SQ):
                        q = b * SQ + q8
                        act.wait_ge(g_mm, i * (2 * SQ) + (q + 3))
                        act.copy(stage[:, b, :, q8 * QUAD:(q8 + 1) * QUAD],
                                 bank[4 + q % 4][:].rearrange("p (t k) -> p k t", t=QUAD)).then_inc(g_out, 1)
                    act.wait_ge(g_out, i * (2 * SQ) + (4 + (b + 1) * SQ))
                    act.dma_start(gdram[:, i * 2 + b], stage[:, b]).then_inc(stage_out[b], 16)

            stages(0, True)
            with act.Fori(1, N_STAGE // 2) as i:
                stages(i, False)

            def experts(g, last):
                for j in range(PER_G):
                    s0 = S_PEER + j
                    if not (last and j + AHEAD >= PER_G):
                        high(s0 + AHEAD, g * PER_G)
                    if j < 8:
                        act.wait_ge(slots_done, g * PER_G + (s0 + 1))
                        act.wait_ge(w_mul, g * 8 + (j + 1))
                        act.activation(ga[:, j % 2, :], bank[j % 2][:, 0:T], ACT.Gelu_apprx_tanh).then_inc(tb_out, 1)

            with act.Fori(0, GROUPS_P - 1) as g:
                experts(g, False)
            experts(GROUPS_P - 1, True)
            deviation(3)

        @block.vector
        def _(dve):
            st = Steps(dve, dve_step)

            def low(s, lap=None):
                r = s % R
                dve.wait_ge(hi_ready, s + 1 if lap is None else lap + (s + 1))
                dve.tensor_tensor(ring_lo[:, r, :], ring_raw[:, r, :], ring_hi[:, r, :].bitcast(F32),
                                  ALU.subtract).then_inc(lo_ready, 1)

            def part(ap, src):
                return dve.tensor_tensor(ap[1], src, ap[0].bitcast(F32), ALU.subtract)

            low(0)
            dve.wait_ge(act_hi, 1)
            part((actT_hi[:], actT_lo[:]), act_raw[:]).then_inc(act_lo, 1)
            low(1)
            low(2)
            dve.wait_ge(act_lo, 1)
            st.done(dve.memset(cmpT_hi[:, :, T:].bitcast(F32), 0.0))
            st.done(dve.memset(cmpT_lo[:, :, T:].bitcast(F32), 0.0))
            st.done(dve.memset(hid_m[:], 0.0))
            for s in range(4):
                low(s + AHEAD)
                dve.wait_ge(tb_out, s + 1)
                part((cmpT_hi[:, s, 0:T], cmpT_lo[:, s, 0:T]), bank[s % 2][:, 0:T]).then_inc(cmp_lo, 1)
            with dve.Fori(1, 8) as i:
                for r in range(4):
                    low(r + AHEAD, i * 4)
            for s in range(S_V, S_GATE + 1):
                low(s + AHEAD)
            dve.wait_ge(gate_exp, 1)
            gflat = gates[:].rearrange("p t h b -> p (t h b)")
            st.done(dve.tensor_scalar(gflat, gflat, 1.0, None, ALU.add))
            st.settle()
            st.done(dve.reciprocal(gflat, gflat))
            dve.wait_ge(pe_split, 1)
            part((pe_hi[:], pe_lo[:]), pe_raw[:]).then_inc(pe_split, 1)
            for s in range(S_CMP, S_CMP + 4):
                low(s + AHEAD)
            dve.wait_ge(hid_ready, 2)
            for h in range(NSA_H):
                g = h // 4
                ins = dve.tensor_copy(hid_m[:, h, 16 * h:16 * h + N_CMP], hidT[:, 1, 16 * g:16 * g + N_CMP])
            ins.then_inc(hidm_ready, 1)
            dve.wait_ge(sc_psum, 1)
            dve.wait_ge(consts, NSA_H)
            st.done(dve.tensor_tensor(zc[:].rearrange("p t h n -> p (t h n)"), bank[0][:, 0:256],
                                      distc[:].rearrange("p t h n -> p (t h n)"), ALU.add))
            st.settle()
            th = lambda ap: ap[:].rearrange("p t h -> p (t h)")
            thn = lambda ap: ap[:].rearrange("p t h n -> p (t h) n")
            wide = lambda ap: th(ap).unsqueeze(2).broadcast_to([P, TT * NSA_H, 16])
            st.done(dve.tensor_reduce(th(mc), thn(zc), AX_X, ALU.max))
            st.settle()
            dve.tensor_tensor(thn(zc), thn(zc), wide(mc), ALU.subtract).then_inc(zc_ready, 1)
            dve.wait_ge(ec_ready, 1)
            st.done(dve.tensor_tensor(thn(pc), thn(pc), thn(maskc), ALU.mult))
            st.settle()
            st.done(dve.tensor_reduce(th(dc), thn(pc), AX_X, ALU.add))
            st.settle()
            st.done(dve.tensor_scalar(th(dc), th(dc), 0.5, None, ALU.max))
            st.settle()
            st.done(dve.reciprocal(th(dc), th(dc)))
            st.settle()
            st.done(dve.tensor_tensor(th(mc), th(dc), gates[:, :, :, 0].rearrange("p t h -> p (t h)"), ALU.mult))
            st.settle()
            st.done(dve.tensor_tensor(thn(pc), thn(pc), wide(mc), ALU.mult))
            st.settle()
            dve.sem_inc(pc_ready, 1)

            units = causal_units()

            def biased(u):
                qb, kb, h, _ = units[u]
                slope = SLOPES[2 * h] if h < NSA_H else SLOPES[2 * (h - NSA_H) + 1]
                dve.wait_ge(s_ready, u + 1)
                if u >= 2:
                    dve.wait_ge(pt_done, u - 1)
                dve.scalar_tensor_tensor(out=z[:, u % 2, :], in0=dist[:], scalar=slope / SCALE, in1=bank[4 + u % 2][:, 0:384],
                                         op0=ALU.mult, op1=ALU.add).then_inc(z_done, 1)
                dve.wait_ge(z_done, u + 1)
                for t, (c0, c1) in enumerate(((0, P), (P, 384))):
                    dve.tensor_reduce(mx[:, u % 2, t:t + 1], z[:, u % 2, c0:c1], AX_X, ALU.max).then_inc(mx_done, 1)
                dve.wait_ge(mx_done, 2 * (u + 1))
                dve.tensor_scalar(nm[:, u % 2, :], mx[:, u % 2, :], -SCALE, None, ALU.mult).then_inc(nm_ready, 1)

            def normed(u):
                h = units[u][2]
                dve.wait_ge(e_done, 2 * (u + 1))
                st.done(dve.reciprocal(rr[:, u % 2, :], rs[:, u % 2, :]))
                st.settle()
                if h < NSA_H:
                    st.done(dve.tensor_tensor(rr[:, u % 2, :], rr[:, u % 2, :], gates[:, :, h, 1 + u % 2], ALU.mult))
                    st.settle()
                for t, (c0, c1) in enumerate(((0, P), (P, 384))):
                    dve.tensor_scalar(z[:, u % 2, c0:c1], z[:, u % 2, c0:c1], rr[:, u % 2, t:t + 1], None,
                                      ALU.mult).then_inc(p_ready, 1)

            def head_low(u):
                h = units[u][2]
                if u >= 2 * NSA_H or u % 2:
                    dve.wait_ge(act_hi, A_X + h + 1)
                    part((actT_hi[:, h, :], actT_lo[:, h, :]), bank[2 + h % 2][:, 0:T]).then_inc(act_lo, 1)

            biased(0)
            for u in range(UNITS + 2):
                if u + 1 < UNITS:
                    biased(u + 1)
                if u < UNITS:
                    normed(u)
                if u >= 2:
                    head_low(u - 2)

            def add_rows(s, bank0, j, scale):
                dve.wait_ge(slots_done, s + 1)
                for t in range(TT):
                    h = hres[:, t, j * 512:(j + 1) * 512]
                    dve.scalar_tensor_tensor(out=h, in0=h, scalar=scale, in1=bank[bank0 + t][:, :], op0=ALU.mult,
                                             op1=ALU.add).then_inc(dve_nb, 1)

            def norm(gbuf_, landed_count):
                for t in range(TT):
                    for j in range(NQ):
                        st.done(dve.bn_stats(stats[:, t, j, :], hres[:, t, j * 512:(j + 1) * 512]))
                st.settle()
                for t in range(TT):
                    st.done(dve.bn_aggr(mv2[:, t, :], stats[:, t].rearrange("p j c -> p (j c)")))
                st.settle()
                st.done(dve.tensor_scalar(rstd[:], mv2[:, :, 1], EPS, None, ALU.add))
                st.settle()
                dve.reciprocal(rstd[:], rstd[:]).then_inc(var_ready, 1)
                dve.wait_ge(rstd_ready, landed_count // 32)
                for t in range(TT):
                    st.done(dve.tensor_scalar(hres[:, t, :], hres[:, t, :], mv2[:, t, 0:1], rstd[:, t:t + 1],
                                              ALU.subtract, ALU.mult))
                dve.wait_ge(gb_landed, landed_count)
                st.settle()
                for t in range(TT):
                    st.done(dve.tensor_tensor(hres[:, t, :], hres[:, t, :], gbuf_[:, 0, :], ALU.mult))
                st.settle()
                for t in range(TT):
                    dve.tensor_tensor(hres[:, t, :], hres[:, t, :], gbuf_[:, 1, :], ALU.add).then_inc(ln_ready, 1)

            def residual_low(hi_first):
                for t in range(TT):
                    for kq in range(4):
                        c = 4 * t + kq
                        dve.wait_ge(act_hi, hi_first + c + 1)
                        sl = (slice(None), slice(4 * kq, 4 * kq + 4), slice(t * P, (t + 1) * P))
                        part((actT_hi[sl], actT_lo[sl]), bank[(6 + c) % 8][:].rearrange("p (k t) -> p k t", k=4)).then_inc(act_lo, 1)

            dve.wait_ge(res_landed, 16)
            for j in range(NQ):
                for q in range(4):
                    s = S_WOUT + 4 * j + q
                    low(s + AHEAD)
                add_rows(s, 2 + 2 * ((3 + j) % 2), j, ALPHA)
            dve.wait_ge(act_hi, A_MEM)
            part((actT_hi[:], actT_lo[:]), mem_raw[:]).then_inc(act_lo, 1)
            low(S_XK + AHEAD)
            dve.wait_ge(dve_nb, 8)
            norm(gb, 32)
            for s in range(S_XK + 1, S_XQ):
                low(s + AHEAD)
            residual_low(A_MEM)
            for s in range(S_XQ, S_XO):
                low(s + AHEAD)
            for h in range(XA_H):
                dve.wait_ge(xs_ready, h + 1)
                st.done(dve.tensor_reduce(xm[:, h, :], bank[2 + h][:].rearrange("p (t k) -> p t k", t=TT), AX_X, ALU.max))
                st.settle()
                dve.tensor_scalar(xm[:, h, :], xm[:, h, :], -SCALE, None, ALU.mult).then_inc(xm_ready, 1)
            for h in range(XA_H):
                dve.wait_ge(xe_done, 2 * (h + 1))
                st.done(dve.reciprocal(xr[:, h, :], xr[:, h, :]))
                st.settle()
                for t in range(TT):
                    dve.tensor_scalar(xp[:, h, t * T:(t + 1) * T], xp[:, h, t * T:(t + 1) * T], xr[:, h, t:t + 1], None,
                                      ALU.mult).then_inc(xp_ready, 1)
            for h in range(XA_H):
                dve.wait_ge(act_hi, A_H1 + h + 1)
                part((actT_hi[:, h, :], actT_lo[:, h, :]), bank[h % 2][:, 0:T]).then_inc(act_lo, 1)
            for j in range(NQ):
                s = S_XO + j
                low(s + AHEAD)
                add_rows(s, 2 + 2 * (j % 2), j, ALPHA)
            dve.wait_ge(dve_nb, 16)
            norm(gb, 64)
            residual_low(A_XO)
            for b in range(16):
                low(S_PQ + b + AHEAD)

            def best16(n, values, work, top, index):
                for b in range(n):
                    st.done(dve.max(top(b, 0), values(b)))
                st.settle()
                for b in range(n):
                    st.done(dve.max_index(index(b, 0), top(b, 0), values(b)))
                    st.done(dve.match_replace(work(b), top(b, 0), values(b), TAKEN))
                st.settle()
                for b in range(n):
                    st.done(dve.max(top(b, 1), work(b)))
                st.settle()
                for b in range(n):
                    st.done(dve.max_index(index(b, 1), top(b, 1), work(b)))
                st.settle()

            for t in range(TT):
                dve.wait_ge(key_out, 2)
                if t:
                    dve.wait_ge(idx_psum, t)
                best16(16, lambda b: sc[:, t, b, :], lambda b: tmp[:, b, :],
                       lambda b, i: sv[:, b, 8 * i:8 * i + 8], lambda b, i: si[:, b, 8 * i:8 * i + 8])
                st.done(dve.tensor_copy(sif[:], si[:]))
                halves = sv[:].rearrange("p (h c) k -> p h c k", c=2)
                for h in range(PEER_H):
                    st.done(dve.tensor_tensor(cand[:, h], halves[:, h, 0, :].unsqueeze(2).broadcast_to([P, TOPK, TOPK]),
                                              halves[:, h, 1, :].unsqueeze(1).broadcast_to([P, TOPK, TOPK]), ALU.add))
                st.settle()
                pairs = lambda h: cand[:, h].rearrange("p i j -> p (i j)")
                spare = tmp[:].rearrange("p (h c) k -> p h (c k)", c=2)
                best16(PEER_H, pairs, lambda h: spare[:, h, :],
                       lambda h, i: tv[:, h, 8 * i:8 * i + 8], lambda h, i: tj[:, h, 8 * i:8 * i + 8])
                st.done(dve.tensor_copy(gsum[:], tv[:, :, 0]))
                st.done(dve.tensor_scalar(tji[:, 0], tj[:], 4, None, ALU.logical_shift_right))
                st.done(dve.tensor_scalar(tji[:, 1], tj[:], TOPK - 1, None, ALU.bitwise_and))
                st.settle()
                st.done(dve.tensor_copy(tjf[:], tji[:]))
                spread = lambda ap: ap.unsqueeze(2).broadcast_to([P, PEER_H, TOPK])
                dve.tensor_tensor(tv[:], tv[:], spread(gsum[:]), ALU.subtract).then_inc(tv_ready, 1)
                st.settle()
                indices = sif[:].rearrange("p (h c) k -> p h c k", c=2)
                count = iota_row[:, 0:TOPK].unsqueeze(1).broadcast_to([P, TOPK, TOPK])
                dve.wait_ge(consts, NSA_H + 1)
                for c in range(2):
                    for h in range(PEER_H):
                        st.done(dve.tensor_tensor(hot[:, h], tjf[:, c, h, :].unsqueeze(2).broadcast_to([P, TOPK, TOPK]),
                                                  count, ALU.is_equal))
                    st.settle()
                    for h in range(PEER_H):
                        st.done(dve.tensor_tensor(hot[:, h], hot[:, h],
                                                  indices[:, h, c, :].unsqueeze(1).broadcast_to([P, TOPK, TOPK]), ALU.mult))
                    st.settle()
                    st.done(dve.tensor_reduce(pick[:, c].rearrange("p h k -> p (h k)"),
                                              hot.rearrange("p h i j -> p (h i) j"), AX_X, ALU.add))
                    st.settle()
                dve.wait_ge(te_done, t + 1)
                st.done(dve.tensor_reduce(gsum[:], pick[:, 2], AX_X, ALU.add))
                st.settle()
                st.done(dve.reciprocal(gsum[:], gsum[:]))
                st.settle()
                dve.tensor_tensor(pick[:, 2], pick[:, 2], spread(gsum[:]), ALU.mult).then_inc(pick_ready, 1)

            dve.wait_ge(ht_done, 16)
            for t in range(TT):
                st.done(dve.tensor_scalar(hres[:, t, :], hres[:, t, :], ALPHA, None, ALU.mult))
            dve.wait_ge(idx_out, 2)
            with dve.Fori(0, N_STAGE // 2) as i:
                for q in range(2 * SQ):
                    n = i * (2 * SQ) + q
                    dve.wait_ge(g_mm, n + 1)
                    for j in range(QUAD):
                        tok = n * QUAD + j
                        ins = dve.tensor_scalar(oh1[:, q % 2, j, :], iota_row[:], idxT[:, 0, bass.ds(tok, 1)],
                                                idxT[:, 2, bass.ds(tok, 1)], ALU.is_equal, ALU.mult)
                    ins.then_inc(oh1_ready, 1)
                    dve.tensor_tensor(oh2[:, q % 2], iota_row[:].unsqueeze(1).broadcast_to([P, QUAD, P]),
                                      idxT[:, 1, bass.ds(n * QUAD, QUAD)].unsqueeze(2).broadcast_to([P, QUAD, P]),
                                      ALU.is_equal).then_inc(oh2_ready, 1)
            st.settle()
            for b in range(2):
                dve.wait_ge(stage_out[b], 16 * (N_STAGE // 2))
            dve.sem_inc(w_mul, 2)

            def experts(g, last):
                for j in range(PER_G):
                    s0 = S_PEER + j
                    if not (last and j + AHEAD >= PER_G):
                        low(s0 + AHEAD, g * PER_G)
                    if j < 8:
                        dve.wait_ge(tb_out, g * 8 + (N_U + j + 1))
                        if j % 4 == 0:
                            dve.wait_ge(g_landed[j // 4], g * 16 + 16)
                        w_eight = lambda ap: ap.rearrange("p (s t) -> p s t", s=N_STAGE)
                        dve.tensor_tensor(w_eight(wt[:, j % 2, :]), w_eight(ga[:, j % 2, :]), gbuf[:, j // 4, :, j % 4, :],
                                          ALU.mult).then_inc(w_mul, 1)
                        dve.wait_ge(w_mul, g * 8 + (j + 3))
                        dve.tensor_copy(w_hi[:, j, :], wt[:, j % 2, :]).then_inc(w_high, 1)
                        dve.wait_ge(w_high, g * 8 + (j + 1))
                        part((w_hi[:, j, :], w_lo[:, j, :]), wt[:, j % 2, :]).then_inc(w_ready, 1)
                    elif j % 2:
                        quarter = (j - 8) // 2
                        dve.wait_ge(slots_done, g * PER_G + (s0 + 1))
                        dve.wait_ge(dve_nb, g * 8 + (8 + 2 * quarter + 2))
                        for t in range(TT):
                            h = hres[:, t, quarter * 512:(quarter + 1) * 512]
                            dve.scalar_tensor_tensor(out=h, in0=h, scalar=1.0, in1=bank[2 + 2 * (quarter % 2) + t][:, :],
                                                     op0=ALU.mult, op1=ALU.add).then_inc(dve_nb, 1)

            with dve.Fori(0, GROUPS_P - 1) as g:
                experts(g, False)
            experts(GROUPS_P - 1, True)
            dve.wait_ge(dve_nb, 16 + 8 * GROUPS_P)
            norm(gb3, 96)


def causal_units():
    units = []
    for h in range(NSA_H):
        g = h // (NSA_H // GROUPS)
        units.append((B_NQ + h, B_KS + g, h, g * HD))
        units.append((B_NQ + h, B_KW + g, h, 256 + g * HD))
    for h in range(MOBA_H):
        units.append((B_MQ + h, B_MK + h, NSA_H + h, 512 + h * HD))
    return units


def lay_out(x):
    import numpy as np

    f = {k: np.asarray(v) for k, v in x.items()}

    def columns(w):
        n = w.shape[1] // P
        return w.reshape(KO, P, n, P).transpose(2, 1, 0, 3).reshape(n, P, KO * P)

    def rows(w):
        q, n = w.shape[0] // 512, w.shape[1] // 512
        return w.reshape(q, 4, P, n, 512).transpose(3, 0, 2, 1, 4).reshape(n * q, P, 2048)

    w = f["w_in"][0]
    c = dict(zip(("nq", "kc", "vc", "ks", "vs", "kw", "vw", "gl", "mq", "mk", "mv"),
                 np.split(w, np.cumsum([1024] + [256] * 6 + [24, 1024, 1024]), axis=1)))
    stream = np.zeros((N_SLOTS, P, 2048), np.float32)
    stream[S_QK:S_V] = columns(np.concatenate([c[n] for n in ("kc", "vc", "ks", "kw", "nq", "mq", "mk")], axis=1))
    stream[S_V:S_GATE] = rows(np.concatenate([c["vs"], c["vw"], c["mv"]], axis=1))
    stream[S_GATE, :, 0:KO * 24] = c["gl"].reshape(KO, P, 24).transpose(1, 0, 2).reshape(P, KO * 24)
    for i, n in enumerate(("cmp_w1_k", "cmp_w1_v")):
        stream[S_CMP + 2 * i:S_CMP + 2 * i + 2] = f[n][0].reshape(2, 16, P, P).transpose(0, 2, 1, 3).reshape(2, P, 2048)
    stream[S_WOUT:S_XK] = rows(f["w_out"][0])
    stream[S_XK:S_XV] = columns(f["xa_wkv"][0][:, 0:512])
    stream[S_XV:S_XQ] = rows(f["xa_wkv"][0][:, 512:1024])
    stream[S_XQ:S_XO] = columns(f["xa_wq"][0])
    stream[S_XO:S_PQ] = rows(f["xa_wo"][0])
    stream[S_PQ:S_PEER] = columns(f["peer_wq"][0])
    peer = stream[S_PEER:].reshape(GROUPS_P, PER_G, P, 2048)
    u = f["peer_u"][0].reshape(GROUPS_P, 8, P, KO, P)
    peer[:, 0:8] = u.transpose(0, 1, 4, 3, 2).reshape(GROUPS_P, 8, P, 2048)
    v = f["peer_v"][0].reshape(GROUPS_P, 2, 4, P, NQ, 512)
    peer[:, 8:16] = v.transpose(0, 4, 1, 3, 2, 5).reshape(GROUPS_P, 8, P, 2048)

    pe = np.zeros((P, 2, 34), np.float32)
    pe[:, 0, 0:32] = f["cmp_pe_k"][0].T
    pe[:, 1, 0:32] = f["cmp_pe_v"][0].T
    turned = lambda z: np.ascontiguousarray(z[0].T.reshape(KO, P, T).transpose(1, 0, 2))
    return {
        "stream": stream,
        "xT": turned(f["x"]),
        "memT": turned(f["mem"]),
        "x": np.ascontiguousarray(f["x"][0].reshape(TT, P, D).transpose(1, 0, 2)),
        "peT": pe,
        "w2": np.ascontiguousarray(np.stack([f["cmp_w2_k"][0], f["cmp_w2_v"][0]], axis=1)),
        "subkT": np.ascontiguousarray(f["peer_subkeys"][0].reshape(16, NKEYS, P).transpose(2, 0, 1)),
        **{f"ln{i}_{n}": np.ascontiguousarray(f[f"ln{i}_{n}"][0]) for i in (1, 2, 3) for n in "gb"},
    }


def kernel(**inputs):
    import concourse.bacc as bacc
    from concourse.bass_utils import run_bass_kernel_spmd

    nc = bacc.Bacc("TRN2", target_bir_lowering=False, num_devices=1)
    arrays = lay_out(inputs)
    aps = {n: nc.dram_tensor(f"in_{n}", v.shape, F32, kind="ExternalInput").ap() for n, v in arrays.items()}
    aps["out"] = nc.dram_tensor("out", (T, D), F32, kind="ExternalOutput").ap()
    build(nc, aps)
    r = run_bass_kernel_spmd(nc, [{f"in_{n}": v for n, v in arrays.items()}], core_ids=[0])
    return r.results[0]["out"].reshape(1, T, D)
```

```python
from contextlib import ExitStack

import concourse.bass as bass
from concourse import mybir

F32 = mybir.dt.float32
F32R = mybir.dt.float32r
U32 = mybir.dt.uint32
ALU = mybir.AluOpType
ACT = mybir.ActivationFunctionType
AX_X = mybir.AxisListType.X

P = 128
T = 256
TT = T // P
D = 2048
KO = D // P
NQ = D // 512
HD = 128
NSA_H, MOBA_H, GROUPS = 8, 8, 2
CMP_STRIDE, CMP_LEN = 16, 32
N_CMP = T // CMP_STRIDE - 1
XA_H = 4
PEER_H, NKEYS, TOPK = 8, 128, 16
SCALE = float(HD) ** -0.5
ALPHA = 2.0 ** 0.25
EPS = 1e-5
MASKED = -1.0e30
TAKEN = -3.0e38
SLOPES = [2.0 ** (-(i + 1) / 2.0) for i in range(16)]

S_KC = 0
S_W1K = 8
S_NQ = 10
S_W1V = 18
S_GATE = 20
S_V = 21
S_MQK = 33
S_WOUT = 49
S_XK = 65
S_XV = 69
S_XQ = 73
S_XO = 77
S_PQ = 81
EARLY_G = 4
S_U0 = 97
S_V0 = S_U0 + 8 * EARLY_G
S_PEER = S_V0 + 8 * EARLY_G
GROUPS_P = 16
LATE_G = GROUPS_P - EARLY_G
PER_G = 16
N_SLOTS = S_PEER + LATE_G * PER_G
R = 4
AHEAD = R - 1

N_NQ, N_GATE, N_MQK, N_XK, N_XQ, N_PQ, N_U = 8, 16, 17, 33, 37, 41, 57

B_KS, B_KW, B_NQ, B_MQ = 0, 2, 4, 12

A_X = 4
A_MIX = A_X + 4
A_MEM = A_MIX + 4
A_H1 = A_MEM + 8
A_XO = A_H1 + XA_H
A_H2 = A_XO + 8

UNITS = 24
DEEP = 3
QUAD = 4
STAGE_T = 16
SQ = STAGE_T // QUAD
N_STAGE = T // STAGE_T
LAPS = 2
LAP_Q = T // QUAD // LAPS
WHILE_LOADING = 4
CHOICE_S = 8 * EARLY_G - 4 * LAPS - WHILE_LOADING


class Steps:

    def __init__(self, eng, sem):
        self.eng, self.sem, self.n = eng, sem, 0

    def done(self, ins):
        ins.then_inc(self.sem, 1)
        self.n += 1

    def settle(self):
        self.eng.wait_ge(self.sem, self.n)


def build(nc, a):
    with ExitStack() as ctx:
        def sb(name, shape, dt=F32, c=ctx):
            return c.enter_context(nc.sbuf_tensor(name, shape, dt))

        def sem(name):
            return ctx.enter_context(nc.semaphore(name))

        bank = [ctx.enter_context(nc.psum_tensor(f"bank{i}", [P, 512], F32)) for i in range(8)]

        ring_raw = sb("ring_raw", [P, R, 2048])
        ring_hi = sb("ring_hi", [P, R, 2048], F32R)
        ring_lo = sb("ring_lo", [P, R, 2048], F32R)
        actT_hi = sb("actT_hi", [P, KO, T], F32R)
        actT_lo = sb("actT_lo", [P, KO, T], F32R)
        ident = sb("ident", [P, P])
        stats = sb("stats", [P, TT, NQ, 6])
        mv2 = sb("mv2", [P, TT, 2])
        rstd = sb("rstd", [P, TT])

        with ExitStack() as c0:
            act_raw = sb("act_raw", [P, KO, T], c=c0)
        with ExitStack() as c0:
            CW = T + 16
            cmpT = sb("cmpT", [P, 4, CW], F32, c0)
            blocks_hl = sb("blocks_hl", [P, CMP_LEN, 2, 32], F32R, c0)
            hidT = sb("hidT", [P, 2, 32], F32, c0)
            hpart = sb("hpart", [P, 2, 32], F32, c0)
            pe_raw = sb("pe_raw", [P, 2, CMP_LEN], F32, c0)
            w2 = sb("w2", [P, 2, P], F32, c0)
        with ExitStack() as c0:
            heads = sb("heads", [P, KO, T], c=c0)
        hres = sb("hres", [P, TT, D])

        with ExitStack() as c1:
            qkT = sb("qkT", [P, 28, T], c=c1)
            vN = sb("vN", [P, TT, 1536], c=c1)
            dist = sb("dist", [P, 384], c=c1)
            distc = sb("distc", [P, TT, NSA_H, 16], c=c1)
            maskc = sb("maskc", [P, TT, NSA_H, 16], c=c1)
            pT = sb("pT", [P, 2, 384], c=c1)
            zc = sb("zc", [P, TT, NSA_H, 16], c=c1)
            pc = sb("pc", [P, TT, NSA_H, 16], c=c1)
            pcT = sb("pcT", [P, T], c=c1)
            vcm = sb("vcm", [P, NSA_H, P], c=c1)
            kcT = sb("kcT", [P, 32], c=c1)
            gates = sb("gates", [P, TT, NSA_H, 3], c=c1)
            mc = sb("mc", [P, TT, NSA_H], c=c1)
            dc = sb("dc", [P, TT, NSA_H], c=c1)
            nm = sb("nm", [P, DEEP, 2], c=c1)
            rs = sb("rs", [P, DEEP, 2], c=c1)
            rr = sb("rr", [P, DEEP, 2], c=c1)
            with ExitStack() as c2:
                blocks = sb("blocks", [P, CMP_LEN, 32], c=c2)
            with ExitStack() as c2:
                hid_m = sb("hid_m", [P, NSA_H, P], F32, c2)
            with ExitStack() as c2:
                z = sb("z", [P, DEEP, 384], c=c2)
            gateT = pcT
        with ExitStack() as c1:
            gb = sb("gb", [P, 2, D], c=c1)
            mem_raw = sb("mem_raw", [P, KO, T], c=c1)
            xk = sb("xk", [P, XA_H, T], c=c1)
            xv = sb("xv", [P, TT, 512], c=c1)
            xq = sb("xq", [P, XA_H, T], c=c1)
            xp = sb("xp", [P, XA_H, 512], c=c1)
            xpT = sb("xpT", [P, 2, 512], c=c1)
            xm = sb("xm", [P, XA_H, 2], c=c1)
            xr = sb("xr", [P, XA_H, 2], c=c1)
        with ExitStack() as c2:
            early = sb("early", [P, 8 * EARLY_G, T], c=c2)
            with ExitStack() as c3:
                idxT = sb("idxT", [P, 3, T], c=c3)
                iota_row = sb("iota_row", [P, P], c=c3)
                with ExitStack() as c4:
                    pq = sb("pq", [P, 16, T], c=c4)
                    sv = sb("sv", [P, 16, TOPK], c=c4)
                    si = sb("si", [P, 16, TOPK], U32, c4)
                    sif = sb("sif", [P, 16, TOPK], F32, c4)
                    tv = sb("tv", [P, TT, PEER_H, TOPK], c=c4)
                    tj = sb("tj", [P, PEER_H, TOPK], U32, c4)
                    tji = sb("tji", [P, 2, PEER_H, TOPK], U32, c4)
                    tjf = sb("tjf", [P, 2, PEER_H, TOPK], F32, c4)
                    pick = sb("pick", [P, TT, 3, PEER_H, TOPK], c=c4)
                    gsum = sb("gsum", [P, TT, PEER_H], c=c4)
                with ExitStack() as c4:
                    oh1 = sb("oh1", [P, 2, QUAD, P], c=c4)
                    oh2 = sb("oh2", [P, 2, QUAD, P], c=c4)
                    stage = sb("stage", [P, 2, P, STAGE_T], c=c4)
            with ExitStack() as c3:
                w_hi = sb("w_hi", [P, 8, T], F32R, c3)
                w_lo = sb("w_lo", [P, 8, T], F32R, c3)
                gbuf = sb("gbuf", [P, 2, N_STAGE, 4, STAGE_T], F32, c3)
                ga = sb("ga", [P, 2, T], c=c3)
                wt = sb("wt", [P, 2, T], c=c3)
        with ExitStack() as c2:
            before_keys = sb("before_keys", [P, 16, T], c=c2)
            subk = sb("subk", [P, 16, P], c=c2)
            sc = sb("sc", [P, 16, P], c=c2)
        with ExitStack() as c2:
            gb3 = sb("gb3", [P, 2, D], c=c2)

        SQUARES = [P, PEER_H, TOPK, TOPK]
        cand = pq[:, 0:8, :].rearrange("p h (i j) -> p h i j", i=TOPK)
        hot = pq[:, 8:16, :].rearrange("p h (i j) -> p h i j", i=TOPK)

        landed = [sem(f"landed{r}") for r in range(R)]
        hi_ready = sem("hi_ready")
        lo_ready = sem("lo_ready")
        slots_done = sem("slots_done")
        tb_out = sem("tb_out")
        blocks_ready = sem("blocks_ready")
        blocks_hi = sem("blocks_hi")
        blocks_lo = sem("blocks_lo")
        hid_part = sem("hid_part")
        hid_sum = sem("hid_sum")
        gate_psum = sem("gate_psum")
        act_nb = sem("act_nb")
        dve_nb = sem("dve_nb")
        x_landed = [sem(f"x_landed{i}") for i in range(4)]
        const_landed = sem("const_landed")
        mem_landed = sem("mem_landed")
        res_landed = sem("res_landed")
        gb_landed = sem("gb_landed")
        subk_landed = sem("subk_landed")
        act_hi = sem("act_hi")
        act_lo = sem("act_lo")
        pool_step = sem("pool_step")
        consts = sem("consts")
        dve_step = sem("dve_step")
        act_step = sem("act_step")
        gate_exp = sem("gate_exp")
        gate_ready = sem("gate_ready")
        head_out = sem("head_out")
        hid_ready = sem("hid_ready")
        hidm_ready = sem("hidm_ready")
        kc_psum = sem("kc_psum")
        kc_ready = sem("kc_ready")
        vc_psum = sem("vc_psum")
        vc_ready = sem("vc_ready")
        sc_psum = sem("sc_psum")
        zc_ready = sem("zc_ready")
        ec_ready = sem("ec_ready")
        pc_ready = sem("pc_ready")
        pct_psum = sem("pct_psum")
        pct_ready = sem("pct_ready")
        s_ready = sem("s_ready")
        z_done = sem("z_done")
        nm_ready = sem("nm_ready")
        e_done = sem("e_done")
        rs_done = sem("rs_done")
        r_ready = sem("r_ready")
        p_ready = sem("p_ready")
        pt_done = sem("pt_done")
        pt_out = sem("pt_out")
        pv_done = sem("pv_done")
        var_ready = sem("var_ready")
        rstd_ready = sem("rstd_ready")
        ln_ready = sem("ln_ready")
        ht_done = sem("ht_done")
        xs_ready = sem("xs_ready")
        xm_ready = sem("xm_ready")
        xe_done = sem("xe_done")
        xp_ready = sem("xp_ready")
        xt_done = sem("xt_done")
        xt_out = sem("xt_out")
        xo_done = sem("xo_done")
        key_psum = sem("key_psum")
        key_out = sem("key_out")
        tv_ready = sem("tv_ready")
        te_done = sem("te_done")
        pick_ready = sem("pick_ready")
        idx_psum = sem("idx_psum")
        idx_out = sem("idx_out")
        oh1_ready = sem("oh1_ready")
        oh2_ready = sem("oh2_ready")
        g_mm = sem("g_mm")
        g_out = sem("g_out")
        stage_out = [sem(f"stage_out{i}") for i in range(2)]
        g_landed = [sem(f"g_landed{i}") for i in range(2)]
        w_mul = sem("w_mul")
        w_high = sem("w_high")
        w_ready = sem("w_ready")
        stored = sem("stored")

        gdram = nc.dram_tensor("gate_matrix", (P, N_STAGE, P, STAGE_T), F32, kind="Internal").ap()

        block = ctx.enter_context(nc.Block())

        @block.sync
        def _(sp):
            for s in range(R):
                k = slice(4 * s, 4 * s + 4)
                sp.dma_start(act_raw[:, k, :], a["xT"][:, k, :]).then_inc(x_landed[s], 16)
                sp.dma_start(ring_raw[:, s, :], a["stream"][s]).then_inc(landed[s], 16)
            rounds = (N_SLOTS - R) // R
            with sp.Fori(0, rounds) as i:
                for r in range(R):
                    sp.wait_ge(lo_ready, i * R + (r + 1))
                    sp.dma_start(ring_raw[:, r, :], a["stream"][i * R + (R + r)]).then_inc(landed[r], 16)
            for s in range(R + rounds * R, N_SLOTS):
                sp.wait_ge(lo_ready, s - R + 1)
                sp.dma_start(ring_raw[:, s % R, :], a["stream"][s]).then_inc(landed[s % R], 16)
            for j in range(NQ):
                sp.wait_ge(ln_ready, 16 + 2 * (j + 1))
                cols = slice(j * 512, (j + 1) * 512)
                sp.dma_start(a["out"].rearrange("(t p) d -> p t d", p=P)[:, :, cols], hres[:, :, cols]).then_inc(stored, 16)
            sp.wait_ge(stored, 16 * NQ)

        @block.gpsimd
        def _(pool):
            st = Steps(pool, pool_step)
            st.done(pool.memset(ident[:], 0.0))
            st.done(pool.iota(dist[:, 0:P], [[1, P]], base=0, channel_multiplier=-1, allow_small_or_imprecise_dtypes=True))
            st.done(pool.iota(dist[:, P:384], [[1, T]], base=-P, channel_multiplier=-1, allow_small_or_imprecise_dtypes=True))
            st.done(pool.iota(distc[:], [[-P, TT], [0, NSA_H], [CMP_STRIDE, 16]], base=CMP_LEN - 1, channel_multiplier=-1,
                              allow_small_or_imprecise_dtypes=True))
            st.done(pool.memset(maskc[:], 1.0))
            st.settle()
            st.done(pool.affine_select(out=ident[:], in_=ident[:], compare_op=ALU.not_equal, fill=1.0, base=0,
                                       pattern=[[-1, P]], channel_multiplier=1))
            st.done(pool.affine_select(out=dist[:, 0:P], in_=dist[:, 0:P], compare_op=ALU.is_ge, fill=MASKED, base=0,
                                       pattern=[[-1, P]], channel_multiplier=1))
            st.done(pool.affine_select(out=dist[:, P:384], in_=dist[:, P:384], compare_op=ALU.is_ge, fill=MASKED, base=P,
                                       pattern=[[-1, T]], channel_multiplier=1))
            for ap, fill in ((distc, MASKED), (maskc, 0.0)):
                st.done(pool.affine_select(out=ap[:], in_=ap[:], compare_op=ALU.is_ge, fill=fill, base=-(CMP_LEN - 1),
                                           pattern=[[P, TT], [0, NSA_H], [-CMP_STRIDE, 16]], channel_multiplier=1))
            st.settle()
            for h in range(NSA_H):
                pool.tensor_scalar(distc[:, :, h, :], distc[:, :, h, :], SLOPES[2 * h], None, ALU.mult).then_inc(consts, 1)
            pool.wait_ge(act_lo, A_X)
            pool.dma_start(pe_raw[:], a["peT"]).then_inc(const_landed, 16)
            pool.dma_start(w2[:], a["w2"]).then_inc(const_landed, 16)
            for u in range(UNITS):
                pool.wait_ge(r_ready, u + 1)
                for t, (c0, c1) in enumerate(((0, P), (P, 384))):
                    pool.tensor_scalar(z[:, u % DEEP, c0:c1], z[:, u % DEEP, c0:c1], rr[:, u % DEEP, t:t + 1], None,
                                       ALU.mult).then_inc(p_ready, 1)
            pool.wait_ge(act_lo, A_MIX)
            pool.dma_start(hres[:], a["x"]).then_inc(res_landed, 16)
            pool.dma_start(mem_raw[:], a["memT"]).then_inc(mem_landed, 16)
            for k in range(2):
                if k:
                    pool.wait_ge(ln_ready, 8)
                for j, name in enumerate((f"ln{k + 1}_g", f"ln{k + 1}_b")):
                    pool.dma_start(gb[:, j, :], a[name].partition_broadcast(P)).then_inc(gb_landed, 16)
            pool.wait_ge(ln_ready, 16)
            pool.dma_start(subk[:], a["subkT"]).then_inc(subk_landed, 16)
            pool.iota(iota_row[:], [[1, P]], base=0, channel_multiplier=0, allow_small_or_imprecise_dtypes=True).then_inc(consts, 1)
            pool.wait_ge(lo_ready, S_U0 + AHEAD)

            def low_instead(s, lap):
                pool.wait_ge(hi_ready, lap + (s + 1))
                pool.tensor_tensor(ring_lo[:, s % R, :], ring_raw[:, s % R, :], ring_hi[:, s % R, :].bitcast(F32),
                                   ALU.subtract).then_inc(lo_ready, 1)

            with pool.Fori(0, 2 * EARLY_G - 1) as i:
                for k in range(4):
                    low_instead(S_U0 + AHEAD + k, i * 4)
            for b in range(2):
                pool.wait_ge(stage_out[b], 16 * (N_STAGE // 2))

            def load_gates(first_key, b):
                pool.dma_start(gbuf[:, b], gdram[:, :, bass.ds(first_key, 4), :]).then_inc(g_landed[b], 16)

            for b in range(2):
                load_gates(4 * b, b)
            for k in range(4):
                low_instead(S_V0 + AHEAD - 4 + k, 0)
            with pool.Fori(1, GROUPS_P) as g:
                for b in range(2):
                    pool.wait_ge(w_mul, g * 8 + (4 * b - 4))
                    load_gates(g * 8 + 4 * b, b)
            for j, name in enumerate(("ln3_g", "ln3_b")):
                pool.dma_start(gb3[:, j, :], a[name].partition_broadcast(P)).then_inc(gb_landed, 16)

        @block.tensor
        def _(pe):
            PASSES = ((0, 0), (0, 1), (1, 0))
            ring = (ring_hi, ring_lo)
            act = (actT_hi, actT_lo)

            def block_slot(s, n, lap=None, fresh=None, tiles=(0, KO)):
                if tiles[0] == 0:
                    pe.wait_ge(lo_ready, s + 1 if lap is None else lap + (s + 1))
                for k in range(*tiles):
                    if fresh and k % 4 == 0:
                        pe.wait_ge(act_lo, fresh[k // 4])
                    for i, (w, x) in enumerate(PASSES):
                        last = pe.matmul(bank[n % 2][:, 0:T], ring[w][:, s % R, k * P:(k + 1) * P], act[x][:, k, :],
                                         start=(k == 0 and i == 0), stop=(k == KO - 1 and i == 2))
                if tiles[1] == KO:
                    last.then_inc(slots_done, 1)

            def row_slot(s, q, nq, outs, fresh=None):
                r = s % R
                pe.wait_ge(lo_ready, s + 1)
                if fresh:
                    pe.wait_ge(act_lo, fresh)
                for t in range(TT):
                    for j in range(4):
                        k = 4 * q + j
                        for n, (x, w) in enumerate(PASSES):
                            last = pe.matmul(outs[t][:, :], act[x][:, k, t * P:(t + 1) * P],
                                             ring[w][:, r, j * 512:(j + 1) * 512],
                                             start=(q == 0 and j == 0 and n == 0),
                                             stop=(q == nq - 1 and j == 3 and n == 2))
                last.then_inc(slots_done, 1)

            def pair(m):
                return bank[2 + 2 * (m % 2)], bank[3 + 2 * (m % 2)]

            for n in range(8):
                if n >= 2:
                    pe.wait_ge(tb_out, n - 1)
                block_slot(S_KC + n, n, fresh=(1, 2, 3, 4) if n == 0 else None)

            def compress(kv):
                out = bank[6 + kv]
                pe.wait_ge(blocks_lo, kv + 1)
                for half in range(2):
                    s = (S_W1K, S_W1V)[kv] + half
                    pe.wait_ge(lo_ready, s + 1)
                    for j in range(16):
                        l = 16 * half + j
                        w = [ring[i][:, s % R, j * P:(j + 1) * P] for i in range(2)]
                        pe.matmul(out[:, 0:64], w[0], blocks_hl[:, l].rearrange("p c n -> p (c n)"), start=(l == 0),
                                  stop=(l == CMP_LEN - 1), skip_group_check=True)
                        last = pe.matmul(out[:, 0:32], w[1], blocks_hl[:, l, 0, :], start=False, stop=(l == CMP_LEN - 1),
                                         skip_group_check=True)
                    last.then_inc(slots_done, 1)

            compress(0)
            for b in range(NSA_H):
                pe.wait_ge(tb_out, N_NQ + b - 1)
                block_slot(S_NQ + b, N_NQ + b)
            pe.wait_ge(const_landed, 32)
            pe.wait_ge(hid_ready, 1)
            pe.matmul(bank[6][:, 128:160], w2[:, 0, :], hidT[:, 0, :], start=True, stop=True).then_inc(kc_psum, 1)
            compress(1)
            pe.wait_ge(tb_out, N_GATE - 1)
            block_slot(S_GATE, N_GATE)
            for q in range(4):
                row_slot(S_V + q, q, 4, pair(0))
            pe.wait_ge(tb_out, N_GATE + 1)
            pe.wait_ge(hid_ready, 2)
            for t in range(TT):
                last = pe.transpose(bank[7][:, t * P:(t + 1) * P], gateT[:, t * P:(t + 1) * P], ident[:])
            last.then_inc(gate_psum, 1)
            pe.wait_ge(kc_ready, 1)
            for t in range(TT):
                for h in range(NSA_H):
                    g = h // (NSA_H // GROUPS)
                    c = (t * NSA_H + h) * 16
                    last = pe.matmul(bank[6][:, c:c + 16], qkT[:, B_NQ + h, t * P:(t + 1) * P], kcT[:, 16 * g:16 * g + 16],
                                     start=True, stop=True)
            last.then_inc(sc_psum, 1)
            for q in range(4):
                row_slot(S_V + 4 + q, q, 4, pair(1))
            pe.wait_ge(act_nb, 2)
            for q in range(4):
                row_slot(S_V + 8 + q, q, 4, pair(2))
            pe.wait_ge(hidm_ready, 1)
            pe.wait_ge(act_nb, 4)
            for h in range(NSA_H):
                last = pe.matmul(bank[4 + h // 4][:, (h % 4) * P:(h % 4 + 1) * P], hid_m[:, h, :], w2[:, 1, :],
                                 start=True, stop=True)
                if h % 4 == 3:
                    last.then_inc(vc_psum, 1)
            pe.wait_ge(pc_ready, 1)
            for t in range(TT):
                last = pe.transpose(bank[7][:, t * P:(t + 1) * P], pc[:, t].rearrange("p h n -> p (h n)"), ident[:])
            last.then_inc(pct_psum, 1)

            units = causal_units()

            def scores(u):
                qb, kb, _, _ = units[u]
                out = bank[4 + u % 2]
                pe.matmul(out[:, 0:P], qkT[:, qb, 0:P], qkT[:, kb, 0:P], start=True, stop=True)
                pe.matmul(out[:, P:384], qkT[:, qb, P:T], qkT[:, kb, :], start=True, stop=True).then_inc(s_ready, 1)

            def turn(u):
                pe.wait_ge(p_ready, 2 * (u + 1))
                if u >= 2:
                    pe.wait_ge(pt_out, u - 1)
                for i in range(3):
                    last = pe.transpose(bank[6 + u % 2][:, i * P:(i + 1) * P], z[:, u % DEEP, i * P:(i + 1) * P], ident[:])
                last.then_inc(pt_done, 1)

            def weigh(u):
                _, _, h, vcol = units[u]
                i, kind = u // 3, u % 3
                out = bank[3 if kind == 2 else 2]
                if i and kind == 0:
                    pe.wait_ge(head_out, 2 * i - 1)
                if i and kind == 2:
                    pe.wait_ge(head_out, 2 * i)
                if kind == 0:
                    pe.matmul(out[:, 0:T], vcm[:, h, :], pcT[:], start=True, stop=False, skip_group_check=True)
                pe.wait_ge(pt_out, u + 1)
                pe.matmul(out[:, 0:T], vN[:, 0, vcol:vcol + P], pT[:, u % 2, 0:T], start=(kind == 2), stop=False,
                          skip_group_check=True)
                pe.matmul(out[:, P:T], vN[:, 1, vcol:vcol + P], pT[:, u % 2, T:384], start=False, stop=True,
                          skip_group_check=True).then_inc(pv_done, 1)

            done = 0

            def moba_blocks(upto):
                nonlocal done
                while done < min(upto, 2 * MOBA_H):
                    pe.wait_ge(tb_out, N_MQK + done - 1)
                    block_slot(S_MQK + done, N_MQK + done)
                    done += 1

            moba_blocks(2)
            pe.wait_ge(vc_ready, 2)
            scores(0)
            scores(1)
            pe.wait_ge(z_done, 1)
            pe.wait_ge(tb_out, N_MQK + 2)
            scores(2)
            pe.wait_ge(pct_ready, 1)
            pe.wait_ge(act_nb, 6)
            for u in range(UNITS):
                moba_blocks(3 + (2 * u + 2) // 3)
                turn(u)
                if u + DEEP < UNITS:
                    pe.wait_ge(z_done, u + 2)
                    if u % 3 == 2:
                        pe.wait_ge(tb_out, N_MQK + 2 * (u // 3) + 4)
                    scores(u + DEEP)
                if u:
                    weigh(u - 1)
            weigh(UNITS - 1)

            for j in range(NQ):
                if j >= 2:
                    pe.wait_ge(dve_nb, 2 * (j - 1))
                for q in range(4):
                    row_slot(S_WOUT + 4 * j + q, q, 4, pair(3 + j), fresh=A_X + q + 1 if j == 0 else None)
            for b in range(XA_H):
                pe.wait_ge(tb_out, N_XK + b - 1)
                block_slot(S_XK + b, N_XK + b, fresh=[A_MIX + 1 + q for q in range(4)] if b == 0 else None)
            pe.wait_ge(dve_nb, 6)

            def turn_residual(kq, banks, ready):
                pe.wait_ge(ln_ready, ready)
                for t in range(TT):
                    for i in range(4):
                        k = 4 * kq + i
                        last = pe.transpose(bank[banks[t]][:, i * P:(i + 1) * P], hres[:, t, k * P:(k + 1) * P], ident[:])
                    last.then_inc(ht_done, 1)

            for q in range(4):
                row_slot(S_XV + q, q, 4, pair(7))
                if q == 0:
                    pe.wait_ge(dve_nb, 8)
                if q >= 2:
                    pe.wait_ge(act_lo, A_MEM + 2 * (q - 1))
                turn_residual(q, HT_BANKS[q % 2], 2 * (q + 1))
            for b in range(XA_H):
                pe.wait_ge(tb_out, N_XQ + b - 1)
                block_slot(S_XQ + b, N_XQ + b, fresh=[A_MEM + 2 * (q + 1) for q in range(4)] if b == 0 else None)
            pe.wait_ge(tb_out, N_PQ)
            pe.wait_ge(act_nb, 8)
            for h in range(XA_H):
                for t in range(TT):
                    last = pe.matmul(bank[2 + h][:, t * T:(t + 1) * T], xq[:, h, t * P:(t + 1) * P], xk[:, h, :],
                                     start=True, stop=True)
                last.then_inc(xs_ready, 1)
            for h in range(XA_H):
                pe.wait_ge(xp_ready, 2 * (h + 1))
                if h >= 2:
                    pe.wait_ge(xt_out, h - 1)
                for kb in range(2):
                    for t in range(TT):
                        c = kb * T + t * P
                        last = pe.transpose(bank[6 + h % 2][:, c:c + P], xp[:, h, t * T + kb * P:t * T + kb * P + P], ident[:])
                last.then_inc(xt_done, 1)
                pe.wait_ge(xt_out, h + 1)
                if h >= 2:
                    pe.wait_ge(act_lo, A_H1 + h - 1)
                for kb in range(2):
                    last = pe.matmul(bank[h % 2][:, 0:T], xv[:, kb, h * HD:(h + 1) * HD], xpT[:, h % 2, kb * T:(kb + 1) * T],
                                     start=(kb == 0), stop=(kb == 1))
                last.then_inc(xo_done, 1)
            pe.wait_ge(act_lo, A_XO)
            for j in range(NQ):
                if j >= 2:
                    pe.wait_ge(dve_nb, 8 + 2 * (j - 1))
                row_slot(S_XO + j, 0, 1, pair(8 + j))
            for q in range(4):
                if q >= 2:
                    pe.wait_ge(act_lo, A_XO + 2 * (q - 1))
                turn_residual(q, HT_BANKS[q % 2], 8 + 2 * (q + 1))
            for b in range(16):
                pe.wait_ge(tb_out, N_PQ + b - 1)
                block_slot(S_PQ + b, N_PQ + b, fresh=[A_XO + 2 * (q + 1) for q in range(4)] if b == 0 else None)
            pe.wait_ge(tb_out, N_U)
            pe.wait_ge(dve_nb, 16)
            pe.wait_ge(subk_landed, 16)
            for t in (1, 0):
                for b in range(16):
                    last = pe.matmul(bank[4 * (1 - t) + b // 4][:, (b % 4) * P:(b % 4 + 1) * P], pq[:, b, t * P:(t + 1) * P],
                                     subk[:, b, :], start=True, stop=True)
                last.then_inc(key_psum, 1)
            pe.wait_ge(key_out, 4)
            with pe.Fori(0, CHOICE_S // 4 - 1) as i:
                for k in range(4):
                    pe.wait_ge(tb_out, i * 4 + (N_U + k - 1))
                    block_slot(S_U0 + k, N_U + k, lap=i * 4)
            for k in range(CHOICE_S - 4, CHOICE_S - 1):
                pe.wait_ge(tb_out, N_U + k - 1)
                block_slot(S_U0 + k, N_U + k)
            for t in range(TT):
                pe.wait_ge(pick_ready, t + 1)
                for c in range(3):
                    last = pe.transpose(bank[2 + t][:, c * P:(c + 1) * P], pick[:, t, c].rearrange("p h k -> p (h k)"), ident[:])
                last.then_inc(idx_psum, 1)
            pe.wait_ge(tb_out, N_U + CHOICE_S - 2)
            block_slot(S_U0 + CHOICE_S - 1, N_U + CHOICE_S - 1)
            pe.sem_inc(g_mm, 2)
            with pe.Fori(0, LAPS) as i:
                for q in range(LAP_Q):
                    n = i * LAP_Q + q
                    pe.wait_ge(oh1_ready, n + 1)
                    pe.wait_ge(oh2_ready, n + 1)
                    pe.wait_ge(g_out, n + 1)
                    for j in range(QUAD):
                        last = pe.matmul(bank[4 + q % 4][:, j * P:(j + 1) * P], oh2[:, q % 2, j, :], oh1[:, q % 2, j, :],
                                         start=True, stop=True)
                    last.then_inc(g_mm, 1)
                    k = CHOICE_S + q // 8
                    if q % 8 == 0:
                        pe.wait_ge(tb_out, i * 4 + (N_U + k - 1))
                    block_slot(S_U0 + k, N_U + k, lap=i * 4, tiles=(2 * (q % 8), 2 * (q % 8) + 2))
            for k in range(8 * EARLY_G - WHILE_LOADING, 8 * EARLY_G):
                pe.wait_ge(tb_out, N_U + k - 1)
                block_slot(S_U0 + k, N_U + k)
            w_part = (w_hi, w_lo)

            def weigh_experts(g, s, lap, chunk0, m0):
                for j in range(NQ):
                    outs = pair(j)
                    pe.wait_ge(dve_nb, g * 8 + (m0 + 2 * (j - 1)))
                    for half in range(2):
                        s0 = s + 2 * j + half
                        pe.wait_ge(lo_ready, g * lap + (s0 + 1))
                        for c4 in range(4):
                            c = 4 * half + c4
                            if j == 0:
                                pe.wait_ge(w_ready, g * 8 + (chunk0 + c + 1))
                            for t in range(TT):
                                for n, (x, w) in enumerate(PASSES):
                                    last = pe.matmul(outs[t][:, :], w_part[x][:, c, t * P:(t + 1) * P],
                                                     ring[w][:, s0 % R, c4 * 512:(c4 + 1) * 512],
                                                     start=(c == 0 and n == 0), stop=(c == 7 and n == 2))
                        last.then_inc(slots_done, 1)

            with pe.Fori(0, EARLY_G) as g:
                weigh_experts(g, S_V0, 8, 0, 16)
            with pe.Fori(0, LATE_G) as g:
                for c in range(8):
                    pe.wait_ge(tb_out, g * 8 + (N_U + 8 * EARLY_G + c - 1))
                    block_slot(S_PEER + c, N_U + c, lap=g * PER_G)
                weigh_experts(g, S_PEER + 8, PER_G, 8 * EARLY_G, 16 + 8 * EARLY_G)

        @block.scalar
        def _(act):
            st = Steps(act, act_step)

            def high(s, lap=None):
                r, laps = s % R, 16 * (s // R + 1)
                act.wait_ge(landed[r], laps if lap is None else lap * (16 // R) + laps)
                if lap is not None:
                    act.wait_ge(slots_done, lap + (s - AHEAD))
                elif s >= R:
                    act.wait_ge(slots_done, s - AHEAD)
                act.copy(ring_hi[:, r, :], ring_raw[:, r, :]).then_inc(hi_ready, 1)

            def deviation(n):
                act.wait_ge(var_ready, n)
                act.activation(rstd[:], rstd[:], ACT.Sqrt).then_inc(rstd_ready, 1)

            def rows_out(s, m, dst):
                act.wait_ge(slots_done, s + 1)
                for t in range(TT):
                    act.copy(dst(t), bank[2 + 2 * (m % 2) + t][:, :]).then_inc(act_nb, 1)

            def block_out(s, n, dst, scale=None, lap=None):
                act.wait_ge(slots_done, s + 1 if lap is None else lap + (s + 1))
                if scale is None:
                    ins = act.copy(dst, bank[n % 2][:, 0:T])
                else:
                    ins = act.mul(dst, bank[n % 2][:, 0:T], scale)
                ins.then_inc(tb_out, 1)

            for k in range(4):
                q = slice(4 * k, 4 * k + 4)
                act.wait_ge(x_landed[k], 16)
                act.copy(actT_hi[:, q, :], act_raw[:, q, :]).then_inc(act_hi, 1)
                if k < AHEAD:
                    high(k)
            for n in range(8):
                high(n + AHEAD)
                if n == 0:
                    act.wait_ge(act_lo, A_X)
                block_out(n, n, cmpT[:, n, 0:T] if n < 4 else qkT[:, n - 4, :])

            def blocks_high(kv):
                act.wait_ge(blocks_ready, kv + 1)
                act.copy(blocks_hl[:, :, 0, :], blocks[:]).then_inc(blocks_hi, 1)

            def hidden(kv):
                act.wait_ge(slots_done, (S_W1K, S_W1V)[kv] + 2)
                act.copy(hpart[:, kv, :], bank[6 + kv][:, 32:64]).then_inc(hid_part, 1)
                act.wait_ge(hid_sum, kv + 1)
                act.activation(hidT[:, kv, :], hpart[:, kv, :], ACT.Gelu_apprx_tanh).then_inc(hid_ready, 1)

            blocks_high(0)
            for s in range(S_W1K, S_NQ):
                high(s + AHEAD)
            hidden(0)
            blocks_high(1)
            for b in range(NSA_H):
                high(S_NQ + b + AHEAD)
                block_out(S_NQ + b, N_NQ + b, qkT[:, B_NQ + b, :], SCALE)
            act.wait_ge(kc_psum, 1)
            act.copy(kcT[:], bank[6][:, 128:160]).then_inc(kc_ready, 1)
            for s in range(S_W1V, S_GATE):
                high(s + AHEAD)
            hidden(1)
            high(S_GATE + AHEAD)
            block_out(S_GATE, N_GATE, gateT[:])
            for s in range(S_V, S_MQK):
                high(s + AHEAD)
                if s == S_V + 4:
                    act.wait_ge(gate_psum, 1)
                    act.activation(gates[:].rearrange("p t h b -> p t (h b)"),
                                   bank[7][:, 0:T].rearrange("p (t c) -> p t c", t=TT)[:, :, 0:24], ACT.Exp,
                                   scale=-1.0).then_inc(gate_exp, 1)
                if s == S_V + 5:
                    act.wait_ge(zc_ready, 1)
                    act.activation(pc[:], zc[:], ACT.Exp).then_inc(ec_ready, 1)
                if (s - S_V) % 4 == 3:
                    m = (s - S_V) // 4
                    rows_out(s, m, lambda t: vN[:, t, 512 * m:512 * (m + 1)])
            for b in range(2):
                act.wait_ge(vc_psum, b + 1)
                act.copy(vcm[:, 4 * b:4 * b + 4, :].rearrange("p h d -> p (h d)"), bank[4 + b][:, :]).then_inc(vc_ready, 1)
            act.wait_ge(pct_psum, 1)
            act.copy(pcT[:], bank[7][:, 0:T]).then_inc(pct_ready, 1)

            units = causal_units()

            def exponentials(u):
                act.wait_ge(nm_ready, u + 1)
                for t, (c0, c1) in enumerate(((0, P), (P, 384))):
                    act.activation(z[:, u % DEEP, c0:c1], z[:, u % DEEP, c0:c1], ACT.Exp, bias=nm[:, u % DEEP, t:t + 1],
                                   accum_out=rs[:, u % DEEP, t:t + 1]).then_inc(e_done, 1)

            def turned_out(u):
                act.wait_ge(pt_done, u + 1)
                if u >= 2:
                    act.wait_ge(pv_done, u - 1)
                act.copy(pT[:, u % 2, :], bank[6 + u % 2][:, 0:384]).then_inc(pt_out, 1)

            def out_of_bank(u):
                h, i, kind = units[u][2], u // 3, u % 3
                if kind:
                    act.wait_ge(pv_done, u + 1)
                    act.copy(heads[:, h, :], bank[3 if kind == 2 else 2][:, 0:T]).then_inc(head_out, 1)

            done = 0

            def moba_blocks(upto):
                nonlocal done
                while done < min(upto, 2 * MOBA_H):
                    high(S_MQK + done + AHEAD)
                    block_out(S_MQK + done, N_MQK + done, qkT[:, B_MQ + done, :], SCALE if done % 2 == 0 else None)
                    done += 1

            moba_blocks(2)
            exponentials(0)
            for u in range(UNITS + 2):
                if 1 <= u <= UNITS:
                    turned_out(u - 1)
                if u + 1 < UNITS:
                    exponentials(u + 1)
                if u >= 2:
                    out_of_bank(u - 2)
                if u < UNITS:
                    moba_blocks(3 + (2 * u + 2) // 3)
            act.wait_ge(slots_done, S_WOUT)
            for k in range(4):
                q = slice(4 * k, 4 * k + 4)
                act.wait_ge(head_out, 16)
                act.copy(actT_hi[:, q, :], heads[:, q, :]).then_inc(act_hi, 1)
            for s in range(S_WOUT, S_XK):
                high(s + AHEAD)
                if s >= S_XK - 4:
                    k = s - (S_XK - 4)
                    q = slice(4 * k, 4 * k + 4)
                    act.wait_ge(mem_landed, 16)
                    act.wait_ge(slots_done, s + 1)
                    act.copy(actT_hi[:, q, :], mem_raw[:, q, :]).then_inc(act_hi, 1)
            high(S_XK + AHEAD)
            deviation(1)
            for b in range(XA_H):
                if b:
                    high(S_XK + b + AHEAD)
                block_out(S_XK + b, N_XK + b, xk[:, b, :])

            def residual_high(kq, first):
                for t in range(TT):
                    act.wait_ge(ht_done, first + 2 * kq + t + 1)
                    act.copy(actT_hi[:, 4 * kq:4 * kq + 4, t * P:(t + 1) * P],
                             bank[HT_BANKS[kq % 2][t]][:].rearrange("p (k t) -> p k t", k=4)).then_inc(act_hi, 1)

            for q in range(4):
                high(S_XV + q + AHEAD)
                act.wait_ge(slots_done, S_XV + q + 1)
                residual_high(q, 0)
            rows_out(S_XV + 3, 7, lambda t: xv[:, t, :])
            for b in range(XA_H):
                high(S_XQ + b + AHEAD)
                block_out(S_XQ + b, N_XQ + b, xq[:, b, :])
            for h in range(XA_H):
                act.wait_ge(xm_ready, h + 1)
                for t in range(TT):
                    act.activation(xp[:, h, t * T:(t + 1) * T], bank[2 + h][:, t * T:(t + 1) * T], ACT.Exp,
                                   bias=xm[:, h, t:t + 1], scale=SCALE, accum_out=xr[:, h, t:t + 1]).then_inc(xe_done, 1)
            for h in range(XA_H):
                act.wait_ge(xt_done, h + 1)
                if h >= 2:
                    act.wait_ge(xo_done, h - 1)
                act.copy(xpT[:, h % 2, :], bank[6 + h % 2][:, :]).then_inc(xt_out, 1)
                act.wait_ge(xo_done, h + 1)
                act.copy(actT_hi[:, h, :], bank[h % 2][:, 0:T]).then_inc(act_hi, 1)
            for j in range(NQ):
                high(S_XO + j + AHEAD)
            deviation(2)
            act.wait_ge(slots_done, S_PQ)
            for q in range(4):
                residual_high(q, 8)
            for b in range(16):
                high(S_PQ + b + AHEAD)
                block_out(S_PQ + b, N_PQ + b, pq[:, b, :])
            act.wait_ge(key_psum, 1)
            for i in range(4):
                act.copy(sc[:, 4 * i:4 * i + 4, :].rearrange("p b k -> p (b k)"), bank[i][:, :]).then_inc(key_out, 1)

            def early_activation(s, n, e, lap):
                high(s + AHEAD, lap)
                act.wait_ge(slots_done, lap + (s + 1))
                act.activation(early[:, e, :], bank[n % 2][:, 0:T], ACT.Gelu_apprx_tanh).then_inc(tb_out, 1)

            with act.Fori(0, CHOICE_S // 4 - 1) as i:
                for k in range(4):
                    early_activation(S_U0 + k, N_U + k, i * 4 + k, i * 4)
            for k in range(CHOICE_S - 4, CHOICE_S):
                early_activation(S_U0 + k, N_U + k, k, 0)
                if k == CHOICE_S - 4:
                    for t in range(TT):
                        act.wait_ge(tv_ready, t + 1)
                        act.activation(pick[:, t, 2], tv[:, t], ACT.Exp).then_inc(te_done, 1)
                if k == CHOICE_S - 2:
                    for t in range(TT):
                        act.wait_ge(idx_psum, t + 1)
                        act.copy(idxT[:, :, t * P:(t + 1) * P],
                                 bank[2 + t][:, 0:384].rearrange("p (c t) -> p c t", c=3)).then_inc(idx_out, 1)
            act.sem_inc(g_out, 4)
            for i in range(LAPS):
                for q in range(LAP_Q):
                    n = i * LAP_Q + q
                    sn, q4 = n // SQ, n % SQ
                    b = sn % 2
                    if q4 == 0 and sn >= 2:
                        act.wait_ge(stage_out[b], 16 * (sn // 2))
                    act.wait_ge(g_mm, n + 3)
                    act.copy(stage[:, b, :, q4 * QUAD:(q4 + 1) * QUAD],
                             bank[4 + q % 4][:].rearrange("p (t k) -> p k t", t=QUAD)).then_inc(g_out, 1)
                    if q4 == SQ - 1:
                        act.wait_ge(g_out, n + 5)
                        act.dma_start(gdram[:, sn], stage[:, b]).then_inc(stage_out[b], 16)
                    if q % 8 == 7:
                        k = CHOICE_S + 4 * i + q // 8
                        early_activation(S_U0 + k, N_U + k, k, 0)
            for k in range(8 * EARLY_G - WHILE_LOADING, 8 * EARLY_G):
                early_activation(S_U0 + k, N_U + k, k, 0)
            with act.Fori(0, EARLY_G) as g:
                for j in range(8):
                    high(S_V0 + j + AHEAD, g * 8)

            def experts(g, last):
                for j in range(PER_G):
                    s0 = S_PEER + j
                    if not (last and j + AHEAD >= PER_G):
                        high(s0 + AHEAD, g * PER_G)
                    if j < 8:
                        act.wait_ge(slots_done, g * PER_G + (s0 + 1))
                        act.wait_ge(w_mul, g * 8 + (8 * EARLY_G + j - 1))
                        act.activation(ga[:, j % 2, :], bank[(N_U + j) % 2][:, 0:T], ACT.Gelu_apprx_tanh).then_inc(tb_out, 1)

            with act.Fori(0, LATE_G - 1) as g:
                experts(g, False)
            experts(LATE_G - 1, True)
            deviation(3)

        @block.vector
        def _(dve):
            st = Steps(dve, dve_step)

            def low(s, lap=None):
                r = s % R
                dve.wait_ge(hi_ready, s + 1 if lap is None else lap + (s + 1))
                dve.tensor_tensor(ring_lo[:, r, :], ring_raw[:, r, :], ring_hi[:, r, :].bitcast(F32),
                                  ALU.subtract).then_inc(lo_ready, 1)

            def part(ap, src):
                return dve.tensor_tensor(ap[1], src, ap[0].bitcast(F32), ALU.subtract)

            for k in range(4):
                q = slice(4 * k, 4 * k + 4)
                dve.wait_ge(act_hi, k + 1)
                part((actT_hi[:, q, :], actT_lo[:, q, :]), act_raw[:, q, :]).then_inc(act_lo, 1)
                if k < AHEAD:
                    low(k)
            dve.wait_ge(act_lo, A_X)
            st.done(dve.memset(cmpT[:, :, T:], 0.0))
            for s in range(4):
                low(s + AHEAD)

            def blocks_sum(kv):
                dve.wait_ge(const_landed, 32)
                for g in range(GROUPS):
                    src = cmpT[:, 2 * kv + g, 0:CW]
                    windows = bass.AP(src.tensor, src.offset, [src.ap[0], [1, CMP_LEN], [CMP_STRIDE, 16]])
                    ins = dve.tensor_tensor(blocks[:, :, 16 * g:16 * g + 16], windows,
                                            pe_raw[:, kv, :].unsqueeze(2).broadcast_to([P, CMP_LEN, 16]), ALU.add)
                    st.done(ins)
                st.settle()
                dve.sem_inc(blocks_ready, 1)

            def blocks_low(kv):
                dve.wait_ge(blocks_hi, kv + 1)
                part((blocks_hl[:, :, 0, :], blocks_hl[:, :, 1, :]), blocks[:]).then_inc(blocks_lo, 1)

            def hidden_sum(kv):
                dve.wait_ge(hid_part, kv + 1)
                dve.tensor_tensor(hpart[:, kv, :], hpart[:, kv, :], bank[6 + kv][:, 0:32], ALU.add).then_inc(hid_sum, 1)

            dve.wait_ge(tb_out, 4)
            st.settle()
            blocks_sum(0)
            for s in range(4, S_W1K):
                low(s + AHEAD)
            blocks_low(0)
            for s in range(S_W1K, S_NQ):
                low(s + AHEAD)
            hidden_sum(0)
            blocks_sum(1)
            blocks_low(1)
            for s in range(S_NQ, S_GATE):
                low(s + AHEAD)
                if s == S_NQ:
                    dve.wait_ge(blocks_lo, 2)
                    st.done(dve.memset(hid_m[:], 0.0))
            hidden_sum(1)
            dve.wait_ge(hid_ready, 2)
            st.settle()
            for h in range(NSA_H):
                g = h // (NSA_H // GROUPS)
                ins = dve.tensor_copy(hid_m[:, h, 16 * h:16 * h + N_CMP], hidT[:, 1, 16 * g:16 * g + N_CMP])
            ins.then_inc(hidm_ready, 1)
            for s in range(S_GATE, S_V + 5):
                low(s + AHEAD)
            dve.wait_ge(gate_exp, 1)
            gflat = gates[:].rearrange("p t h b -> p (t h b)")
            st.done(dve.tensor_scalar(gflat, gflat, 1.0, None, ALU.add))
            st.settle()
            st.done(dve.reciprocal(gflat, gflat))
            dve.wait_ge(sc_psum, 1)
            dve.wait_ge(consts, NSA_H)
            st.done(dve.tensor_tensor(zc[:].rearrange("p t h n -> p (t h n)"), bank[6][:, 0:256],
                                      distc[:].rearrange("p t h n -> p (t h n)"), ALU.add))
            st.settle()
            th = lambda ap: ap[:].rearrange("p t h -> p (t h)")
            thn = lambda ap: ap[:].rearrange("p t h n -> p (t h) n")
            wide = lambda ap: th(ap).unsqueeze(2).broadcast_to([P, TT * NSA_H, 16])
            st.done(dve.tensor_reduce(th(mc), thn(zc), AX_X, ALU.max))
            st.settle()
            dve.tensor_tensor(thn(zc), thn(zc), wide(mc), ALU.subtract).then_inc(zc_ready, 1)
            low(S_V + 5 + AHEAD)
            dve.wait_ge(ec_ready, 1)
            st.done(dve.tensor_tensor(thn(pc), thn(pc), thn(maskc), ALU.mult))
            st.settle()
            st.done(dve.tensor_reduce(th(dc), thn(pc), AX_X, ALU.add))
            st.settle()
            st.done(dve.tensor_scalar(th(dc), th(dc), 0.5, None, ALU.max))
            st.settle()
            st.done(dve.reciprocal(th(dc), th(dc)))
            st.settle()
            st.done(dve.tensor_tensor(th(mc), th(dc), gates[:, :, :, 0].rearrange("p t h -> p (t h)"), ALU.mult))
            st.settle()
            st.done(dve.tensor_tensor(thn(pc), thn(pc), wide(mc), ALU.mult))
            st.settle()
            dve.sem_inc(pc_ready, 1)
            for s in range(S_V + 6, S_MQK):
                low(s + AHEAD)

            units = causal_units()

            def biased(u):
                h = units[u][2]
                slope = SLOPES[2 * h] if h < NSA_H else SLOPES[2 * (h - NSA_H) + 1]
                dve.wait_ge(s_ready, u + 1)
                if u >= DEEP:
                    dve.wait_ge(pt_done, u - DEEP + 1)
                dve.scalar_tensor_tensor(out=z[:, u % DEEP, :], in0=dist[:], scalar=slope, in1=bank[4 + u % 2][:, 0:384],
                                         op0=ALU.mult, op1=ALU.add).then_inc(z_done, 1)
                dve.wait_ge(z_done, u + 1)
                for t, (c0, c1) in enumerate(((0, P), (P, 384))):
                    ins = dve.tensor_reduce(nm[:, u % DEEP, t:t + 1], z[:, u % DEEP, c0:c1], AX_X, ALU.max, negate=True)
                ins.then_inc(nm_ready, 1)

            def normed(u):
                h = units[u][2]
                dve.wait_ge(e_done, 2 * (u + 1))
                if u >= DEEP:
                    dve.wait_ge(p_ready, 2 * (u - DEEP + 1))
                ins = dve.reciprocal(rr[:, u % DEEP, :], rs[:, u % DEEP, :])
                if h < NSA_H:
                    st.done(ins)
                    st.settle()
                    ins = dve.tensor_tensor(rr[:, u % DEEP, :], rr[:, u % DEEP, :], gates[:, :, h, 1 + u % 3], ALU.mult)
                ins.then_inc(r_ready, 1)

            done = 0

            def moba_blocks(upto):
                nonlocal done
                while done < min(upto, 2 * MOBA_H):
                    low(S_MQK + done + AHEAD)
                    done += 1

            moba_blocks(2)
            biased(0)
            biased(1)
            normed(0)
            for u in range(UNITS):
                if u + 2 < UNITS:
                    biased(u + 2)
                if u + 1 < UNITS:
                    normed(u + 1)
                moba_blocks(3 + (2 * u + 2) // 3)

            def add_rows(s, bank0, j, scale, nb, stat):
                for t in range(TT):
                    h = hres[:, t, j * 512:(j + 1) * 512]
                    dve.scalar_tensor_tensor(out=h, in0=h, scalar=scale, in1=bank[bank0 + t][:, :], op0=ALU.mult,
                                             op1=ALU.add).then_inc(dve_nb, 1)
                if stat:
                    dve.wait_ge(dve_nb, nb)
                    for t in range(TT):
                        st.done(dve.bn_stats(stats[:, t, j, :], hres[:, t, j * 512:(j + 1) * 512]))

            def norm(gains, n, meanwhile=()):
                spare = list(meanwhile)
                st.settle()
                for t in range(TT):
                    st.done(dve.bn_aggr(mv2[:, t, :], stats[:, t].rearrange("p j c -> p (j c)")))
                st.settle()
                st.done(dve.tensor_scalar(rstd[:], mv2[:, :, 1], EPS, None, ALU.add))
                st.settle()
                dve.reciprocal(rstd[:], rstd[:]).then_inc(var_ready, 1)
                if spare:
                    spare.pop(0)()
                dve.wait_ge(gb_landed, 32 * n)
                for j in range(NQ + 1):
                    if j == 1:
                        dve.wait_ge(rstd_ready, n)
                    marked = st.n
                    if j < NQ:
                        c = slice(j * 512, (j + 1) * 512)
                        for t in range(TT):
                            st.done(dve.scalar_tensor_tensor(out=hres[:, t, c], in0=hres[:, t, c], scalar=mv2[:, t, 0:1],
                                                             in1=gains[:, 0, c], op0=ALU.subtract, op1=ALU.mult))
                    if j:
                        c = slice((j - 1) * 512, j * 512)
                        dve.wait_ge(dve_step, marked)
                        for t in range(TT):
                            dve.scalar_tensor_tensor(out=hres[:, t, c], in0=hres[:, t, c], scalar=rstd[:, t:t + 1],
                                                     in1=gains[:, 1, c], op0=ALU.mult, op1=ALU.add).then_inc(ln_ready, 1)
                    if spare and j == 2:
                        spare.pop(0)()

            def residual_low(kq, hi_first):
                for t in range(TT):
                    dve.wait_ge(act_hi, hi_first + 2 * kq + t + 1)
                    sl = (slice(None), slice(4 * kq, 4 * kq + 4), slice(t * P, (t + 1) * P))
                    part((actT_hi[sl], actT_lo[sl]),
                         bank[HT_BANKS[kq % 2][t]][:].rearrange("p (k t) -> p k t", k=4)).then_inc(act_lo, 1)

            for k in range(4):
                q = slice(4 * k, 4 * k + 4)
                dve.wait_ge(act_hi, A_X + k + 1)
                part((actT_hi[:, q, :], actT_lo[:, q, :]), heads[:, q, :]).then_inc(act_lo, 1)
            for j in range(NQ):
                for q in range(4):
                    s = S_WOUT + 4 * j + q
                    low(s + AHEAD)
                    if j == NQ - 1:
                        k = slice(4 * q, 4 * q + 4)
                        dve.wait_ge(act_hi, A_MIX + q + 1)
                        part((actT_hi[:, k, :], actT_lo[:, k, :]), mem_raw[:, k, :]).then_inc(act_lo, 1)
                dve.wait_ge(slots_done, s + 1)
                dve.wait_ge(res_landed, 16)
                add_rows(s, 2 + 2 * ((3 + j) % 2), j, ALPHA, 2 * (j + 1), True)
            norm(gb, 1, [lambda: low(S_XK + AHEAD), lambda: low(S_XK + 1 + AHEAD)])
            for s in range(S_XK + 2, S_XV):
                low(s + AHEAD)
            for q in range(4):
                low(S_XV + q + AHEAD)
                residual_low(q, A_MEM)
            for s in range(S_XQ, S_XO):
                low(s + AHEAD)
            for h in range(XA_H):
                dve.wait_ge(xs_ready, h + 1)
                st.done(dve.tensor_reduce(xm[:, h, :], bank[2 + h][:].rearrange("p (t k) -> p t k", t=TT), AX_X, ALU.max))
                st.settle()
                dve.tensor_scalar(xm[:, h, :], xm[:, h, :], -SCALE, None, ALU.mult).then_inc(xm_ready, 1)
            for h in range(XA_H):
                dve.wait_ge(xe_done, 2 * (h + 1))
                st.done(dve.reciprocal(xr[:, h, :], xr[:, h, :]))
                st.settle()
                for t in range(TT):
                    dve.tensor_scalar(xp[:, h, t * T:(t + 1) * T], xp[:, h, t * T:(t + 1) * T], xr[:, h, t:t + 1], None,
                                      ALU.mult).then_inc(xp_ready, 1)
            for h in range(XA_H):
                dve.wait_ge(act_hi, A_H1 + h + 1)
                part((actT_hi[:, h, :], actT_lo[:, h, :]), bank[h % 2][:, 0:T]).then_inc(act_lo, 1)
            for j in range(NQ):
                s = S_XO + j
                low(s + AHEAD)
                dve.wait_ge(slots_done, s + 1)
                add_rows(s, 2 + 2 * (j % 2), j, ALPHA, 8 + 2 * (j + 1), True)
            norm(gb, 2)
            for q in range(4):
                residual_low(q, A_XO)
            for b in range(16):
                low(S_PQ + b + AHEAD)

            def best16(n, values, top, index):
                for b in range(n):
                    st.done(dve.max(top(b, 0), values(b)))
                st.settle()
                for b in range(n):
                    st.done(dve.max_index(index(b, 0), top(b, 0), values(b)))
                for b in range(n):
                    st.done(dve.match_replace(values(b), top(b, 0), values(b), TAKEN))
                st.settle()
                for b in range(n):
                    st.done(dve.max(top(b, 1), values(b)))
                st.settle()
                for b in range(n):
                    st.done(dve.max_index(index(b, 1), top(b, 1), values(b)))
                st.settle()

            for t in range(TT):
                dve.wait_ge(key_psum, 2)
                dve.wait_ge(key_out, 4)
                best16(16, lambda b: sc[:, b, :] if t else bank[4 + b // 4][:, (b % 4) * P:(b % 4 + 1) * P],
                       lambda b, i: sv[:, b, 8 * i:8 * i + 8], lambda b, i: si[:, b, 8 * i:8 * i + 8])
                st.done(dve.tensor_copy(sif[:], si[:]))
                halves = sv[:].rearrange("p (h c) k -> p h c k", c=2)
                st.done(dve.tensor_tensor(cand, halves[:, :, 0, :].unsqueeze(3).broadcast_to(SQUARES),
                                          halves[:, :, 1, :].unsqueeze(2).broadcast_to(SQUARES), ALU.add))
                st.settle()
                pairs = lambda h: cand[:, h].rearrange("p i j -> p (i j)")
                best16(PEER_H, pairs,
                       lambda h, i: tv[:, t, h, 8 * i:8 * i + 8], lambda h, i: tj[:, h, 8 * i:8 * i + 8])
                st.done(dve.tensor_copy(gsum[:, t], tv[:, t, :, 0]))
                st.done(dve.tensor_scalar(tji[:, 0], tj[:], 4, None, ALU.logical_shift_right))
                st.done(dve.tensor_scalar(tji[:, 1], tj[:], TOPK - 1, None, ALU.bitwise_and))
                st.settle()
                st.done(dve.tensor_copy(tjf[:], tji[:]))
                spread = lambda ap: ap.unsqueeze(2).broadcast_to([P, PEER_H, TOPK])
                dve.tensor_tensor(tv[:, t], tv[:, t], spread(gsum[:, t]), ALU.subtract).then_inc(tv_ready, 1)
                st.settle()
                indices = sif[:].rearrange("p (h c) k -> p h c k", c=2)
                count = iota_row[:, 0:TOPK].unsqueeze(1).unsqueeze(1).broadcast_to(SQUARES)
                dve.wait_ge(consts, NSA_H + 1)
                for c in range(2):
                    st.done(dve.tensor_tensor(hot, tjf[:, c].unsqueeze(3).broadcast_to(SQUARES), count, ALU.is_equal))
                    st.settle()
                    st.done(dve.tensor_tensor(hot, hot, indices[:, :, c, :].unsqueeze(2).broadcast_to(SQUARES), ALU.mult))
                    st.settle()
                    st.done(dve.tensor_reduce(pick[:, t, c].rearrange("p h k -> p (h k)"),
                                              hot.rearrange("p h i j -> p (h i) j"), AX_X, ALU.add))
                    st.settle()
            dve.wait_ge(te_done, TT)
            for t in range(TT):
                st.done(dve.tensor_reduce(gsum[:, t], pick[:, t, 2], AX_X, ALU.add))
            st.settle()
            st.done(dve.reciprocal(gsum[:], gsum[:]))
            st.settle()
            for t in range(TT):
                dve.tensor_tensor(pick[:, t, 2], pick[:, t, 2], spread(gsum[:, t]), ALU.mult).then_inc(pick_ready, 1)

            dve.wait_ge(ht_done, 16)
            for t in range(TT):
                st.done(dve.tensor_scalar(hres[:, t, :], hres[:, t, :], ALPHA, None, ALU.mult))
            dve.wait_ge(idx_out, 2)
            with dve.Fori(0, LAPS) as i:
                for q in range(LAP_Q):
                    n = i * LAP_Q + q
                    dve.wait_ge(g_mm, n + 1)
                    for j in range(QUAD):
                        tok = n * QUAD + j
                        ins = dve.tensor_scalar(oh1[:, q % 2, j, :], iota_row[:], idxT[:, 0, bass.ds(tok, 1)],
                                                idxT[:, 2, bass.ds(tok, 1)], ALU.is_equal, ALU.mult)
                    ins.then_inc(oh1_ready, 1)
                    dve.tensor_tensor(oh2[:, q % 2], iota_row[:].unsqueeze(1).broadcast_to([P, QUAD, P]),
                                      idxT[:, 1, bass.ds(n * QUAD, QUAD)].unsqueeze(2).broadcast_to([P, QUAD, P]),
                                      ALU.is_equal).then_inc(oh2_ready, 1)
            st.settle()
            for b in range(2):
                dve.wait_ge(stage_out[b], 16 * (N_STAGE // 2))

            def gated(src, g, c, chunk0):
                if c % 4 == 0:
                    dve.wait_ge(g_landed[c // 4], g * 16 + (16 + 2 * chunk0))
                staged = lambda ap: ap.rearrange("p (s t) -> p s t", s=N_STAGE)
                dve.tensor_tensor(staged(wt[:, c % 2, :]), staged(src), gbuf[:, c // 4, :, c % 4, :], ALU.mult).then_inc(w_mul, 1)
                dve.wait_ge(w_mul, g * 8 + (chunk0 + c + 1))
                dve.tensor_copy(w_hi[:, c, :], wt[:, c % 2, :]).then_inc(w_high, 1)
                dve.wait_ge(w_high, g * 8 + (chunk0 + c + 1))
                part((w_hi[:, c, :], w_lo[:, c, :]), wt[:, c % 2, :]).then_inc(w_ready, 1)

            def add_experts(g, s, lap, j, nb0, stat=False):
                dve.wait_ge(slots_done, g * lap + (s + 1))
                dve.wait_ge(dve_nb, g * 8 + (nb0 + 2 * j - 6))
                add_rows(s, 2 + 2 * (j % 2), j, 1.0, nb0 + 8 * g + 2 * (j + 1) if stat else None, stat)

            for g in range(EARLY_G):
                for j in range(8):
                    s = S_V0 + 8 * g + j
                    if g == 0 and j == 0:
                        for c in range(4):
                            gated(early[:, c, :], 0, c, 0)
                    if j == 0:
                        dve.wait_ge(tb_out, N_U + 8 * (g + 1))
                        if g:
                            dve.wait_ge(slots_done, s)
                        for c in range(4, 8):
                            gated(early[:, 8 * g + c, :], 0, c, 8 * g)
                    if g == 0 and j == 0:
                        dve.wait_ge(lo_ready, S_V0 + AHEAD)
                    low(s + AHEAD)
                    if j == 7 and g + 1 < EARLY_G:
                        dve.wait_ge(slots_done, s)
                        dve.wait_ge(tb_out, N_U + 8 * (g + 2))
                        for c in range(4):
                            gated(early[:, 8 * (g + 1) + c, :], 0, c, 8 * (g + 1))
                    if j % 2:
                        add_experts(0, s, 0, j // 2, 16 + 8 * g)

            def experts(g, last):
                for j in range(PER_G):
                    s0 = S_PEER + j
                    if not (last and j + AHEAD >= PER_G):
                        low(s0 + AHEAD, g * PER_G)
                    if j < 8:
                        dve.wait_ge(tb_out, g * 8 + (N_U + 8 * EARLY_G + j + 1))
                        gated(ga[:, j % 2, :], g, j, 8 * EARLY_G)
                    elif j % 2:
                        add_experts(g, s0, PER_G, (j - 8) // 2, 16 + 8 * EARLY_G, last)

            with dve.Fori(0, LATE_G - 1) as g:
                experts(g, False)
            experts(LATE_G - 1, True)
            norm(gb3, 3)


HT_BANKS = ((6, 7), (2, 3))


def causal_units():
    units = []
    for h in range(NSA_H):
        g = h // (NSA_H // GROUPS)
        units.append((B_NQ + h, B_KS + g, h, g * HD))
        units.append((B_NQ + h, B_KW + g, h, 256 + g * HD))
        units.append((B_MQ + 2 * h, B_MQ + 2 * h + 1, NSA_H + h, 512 + h * HD))
    return units


def lay_out(x):
    import numpy as np

    f = {k: np.asarray(v) for k, v in x.items()}

    def columns(w):
        n = w.shape[1] // P
        return w.reshape(KO, P, n, P).transpose(2, 1, 0, 3).reshape(n, P, KO * P)

    def rows(w):
        q, n = w.shape[0] // 512, w.shape[1] // 512
        return w.reshape(q, 4, P, n, 512).transpose(3, 0, 2, 1, 4).reshape(n * q, P, 2048)

    w = f["w_in"][0]
    c = dict(zip(("nq", "kc", "vc", "ks", "vs", "kw", "vw", "gl", "mq", "mk", "mv"),
                 np.split(w, np.cumsum([1024] + [256] * 6 + [24, 1024, 1024]), axis=1)))
    stream = np.zeros((N_SLOTS, P, 2048), np.float32)
    stream[S_KC:S_W1K] = columns(np.concatenate([c[n] for n in ("kc", "vc", "ks", "kw")], axis=1))
    stream[S_NQ:S_W1V] = columns(c["nq"])
    stream[S_GATE].reshape(P, KO, P)[:, :, 0:24] = c["gl"].reshape(KO, P, 24).transpose(1, 0, 2)
    stream[S_V:S_MQK] = rows(np.concatenate([c["vs"], c["vw"], c["mv"]], axis=1))
    stream[S_MQK:S_WOUT:2] = columns(c["mq"])
    stream[S_MQK + 1:S_WOUT:2] = columns(c["mk"])
    for s, n in ((S_W1K, "cmp_w1_k"), (S_W1V, "cmp_w1_v")):
        stream[s:s + 2] = f[n][0].reshape(2, 16, P, P).transpose(0, 2, 1, 3).reshape(2, P, 2048)
    stream[S_WOUT:S_XK] = rows(f["w_out"][0])
    stream[S_XK:S_XV] = columns(f["xa_wkv"][0][:, 0:512])
    stream[S_XV:S_XQ] = rows(f["xa_wkv"][0][:, 512:1024])
    stream[S_XQ:S_XO] = columns(f["xa_wq"][0])
    stream[S_XO:S_PQ] = rows(f["xa_wo"][0])
    stream[S_PQ:S_U0] = columns(f["peer_wq"][0])
    u = f["peer_u"][0].reshape(GROUPS_P, 8, P, KO, P).transpose(0, 1, 4, 3, 2).reshape(GROUPS_P, 8, P, 2048)
    v = f["peer_v"][0].reshape(GROUPS_P, 2, 4, P, NQ, 512).transpose(0, 4, 1, 3, 2, 5).reshape(GROUPS_P, 8, P, 2048)
    stream[S_U0:S_V0] = u[:EARLY_G].reshape(-1, P, 2048)
    stream[S_V0:S_PEER] = v[:EARLY_G].reshape(-1, P, 2048)
    peer = stream[S_PEER:].reshape(LATE_G, PER_G, P, 2048)
    peer[:, 0:8] = u[EARLY_G:]
    peer[:, 8:16] = v[EARLY_G:]

    pe = np.ascontiguousarray(np.stack([f["cmp_pe_k"][0].T, f["cmp_pe_v"][0].T], axis=1))
    turned = lambda z: np.ascontiguousarray(z[0].T.reshape(KO, P, T).transpose(1, 0, 2))
    return {
        "stream": stream,
        "xT": turned(f["x"]),
        "memT": turned(f["mem"]),
        "x": np.ascontiguousarray(f["x"][0].reshape(TT, P, D).transpose(1, 0, 2)),
        "peT": pe,
        "w2": np.ascontiguousarray(np.stack([f["cmp_w2_k"][0], f["cmp_w2_v"][0]], axis=1)),
        "subkT": np.ascontiguousarray(f["peer_subkeys"][0].reshape(16, NKEYS, P).transpose(2, 0, 1)),
        **{f"ln{i}_{n}": np.ascontiguousarray(f[f"ln{i}_{n}"][0]) for i in (1, 2, 3) for n in "gb"},
    }


def kernel(**inputs):
    import concourse.bacc as bacc
    from concourse.bass_utils import run_bass_kernel_spmd

    nc = bacc.Bacc("TRN2", target_bir_lowering=False, num_devices=1)
    arrays = lay_out(inputs)
    aps = {n: nc.dram_tensor(f"in_{n}", v.shape, F32, kind="ExternalInput").ap() for n, v in arrays.items()}
    aps["out"] = nc.dram_tensor("out", (T, D), F32, kind="ExternalOutput").ap()
    build(nc, aps)
    r = run_bass_kernel_spmd(nc, [{f"in_{n}": v for n, v in arrays.items()}], core_ids=[0])
    return r.results[0]["out"].reshape(1, T, D)
```
